# Optimizing a Trainium2 kernel written in Bass

```python
import math
import jax, jax.numpy as jnp
from jax import lax
import numpy as np

D_MODEL = 1024
BATCH = 1
SEQ = 512
DEPTH = 1
DEC_BATCH = 1
DEC_SEQ = 512
PAST_LEN = 128

RET_HEADS = 4
RET_DK = 128
RET_DV = 256
RET_CHUNK = 128
ATT_GROUPS = ((128, 1), (512, 4), (2048, 16))
ATT_HEADS_PER_GROUP = 8
ATT_HEADS = ATT_HEADS_PER_GROUP * len(ATT_GROUPS)
ATT_DH = 64
N_EXPERTS = 16
EC_CAPACITY_FACTOR = 2
EXPERT_HIDDEN = 2048
ROPE_THETA = 10000.0
EPS = 1e-6
N_BRANCHES = 2

RQ = RET_HEADS * RET_DK
RV = RET_HEADS * RET_DV
AQ = ATT_HEADS * ATT_DH
A_OUT = ATT_HEADS_PER_GROUP * ATT_DH
IN_COLS = 2 * RQ + 2 * RV + 3 * AQ + N_BRANCHES * D_MODEL

kernel_name = "hybrid_retention_dilated_attn_ec_moe_encoder"

def rmsnorm(x, gain):
    x32 = x.astype(jnp.float32)
    y = x32 * lax.rsqrt(jnp.mean(x32 * x32, axis=-1, keepdims=True) + EPS)
    return (y * gain.astype(jnp.float32)).astype(x.dtype)

def rotate(x, inv_freq):
    T = x.shape[1]
    pos = jnp.arange(T, dtype=jnp.float32)
    ang = pos[:, None] * inv_freq[None, :]
    cos = jnp.cos(ang)[None, :, None, :]
    sin = jnp.sin(ang)[None, :, None, :]
    x32 = x.astype(jnp.float32)
    x1, x2 = jnp.split(x32, 2, axis=-1)
    return jnp.concatenate([x1 * cos - x2 * sin, x2 * cos + x1 * sin], axis=-1).astype(x.dtype)

def retention_one_direction(q, k, v, log_gamma, include_diag):
    B, H, T, dk = q.shape
    dv = v.shape[-1]
    C = RET_CHUNK
    N = T // C
    lg = log_gamma.astype(jnp.float32)
    qc = q.reshape(B, H, N, C, dk)
    kc = k.reshape(B, H, N, C, dk)
    vc = v.reshape(B, H, N, C, dv)
    idx = jnp.arange(C, dtype=jnp.float32)
    diff = idx[:, None] - idx[None, :]
    mask = (diff >= 0) if include_diag else (diff > 0)
    decay = jnp.where(mask[None], jnp.exp(lg[:, None, None] * jnp.where(mask, diff, 0.0)[None]), 0.0)
    scores = jnp.einsum('bhncd,bhnsd->bhncs', qc, kc) * decay[None, :, None]
    out_inner = jnp.einsum('bhncs,bhnse->bhnce', scores, vc)
    k_dec = kc * jnp.exp(lg[:, None] * (C - 1 - idx)[None, :])[None, :, None, :, None]
    kv = jnp.einsum('bhncd,bhnce->nbhde', k_dec, vc)
    chunk_decay = jnp.exp(lg * C)[None, :, None, None]

    def step(state, kv_n):
        return state * chunk_decay + kv_n, state

    init = jnp.zeros((B, H, dk, dv), kv.dtype)
    _, states = lax.scan(step, init, kv)
    q_dec = qc * jnp.exp(lg[:, None] * (idx + 1.0)[None, :])[None, :, None, :, None]
    out_cross = jnp.einsum('bhncd,nbhde->bhnce', q_dec, states)
    return (out_inner + out_cross).reshape(B, H, T, dv)

def dilated_group_attention(q, k, v, window, dil):
    B, T, Hg, dh = q.shape
    L = T // dil
    n = window // (2 * dil)
    QB = n
    nb = -(-L // QB)
    Lp = nb * QB

    def to_sub(x):
        return x.reshape(B, L, dil, Hg, dh).transpose(0, 2, 3, 1, 4)

    qs, ks, vs = to_sub(q), to_sub(k), to_sub(v)
    qp = jnp.pad(qs, ((0, 0), (0, 0), (0, 0), (0, Lp - L), (0, 0)))
    kv_pad = ((0, 0), (0, 0), (0, 0), (n, Lp - L + n), (0, 0))
    kp = jnp.pad(ks, kv_pad).reshape(B, dil, Hg, nb + 2, QB, dh)
    vp = jnp.pad(vs, kv_pad).reshape(B, dil, Hg, nb + 2, QB, dh)
    kwin = jnp.concatenate([kp[:, :, :, :-2], kp[:, :, :, 1:-1], kp[:, :, :, 2:]], axis=4)
    vwin = jnp.concatenate([vp[:, :, :, :-2], vp[:, :, :, 1:-1], vp[:, :, :, 2:]], axis=4)
    qb = qp.reshape(B, dil, Hg, nb, QB, dh)
    s = jnp.einsum('brhnqe,brhnke->brhnqk', qb, kwin).astype(jnp.float32)
    qq = jnp.arange(QB)
    kk = jnp.arange(3 * QB)
    blk = jnp.arange(nb)
    band = jnp.abs(kk[None, :] - n - qq[:, None]) <= n
    key_pos = blk[:, None] * QB - n + kk[None, :]
    valid = (key_pos >= 0) & (key_pos < L)
    mask = band[None] & valid[:, None, :]
    s = jnp.where(mask[None, None, None], s, -jnp.inf)
    m = jnp.max(s, axis=-1)
    p = jnp.exp(s - m[..., None])
    l = jnp.sum(p, axis=-1)
    acc = jnp.einsum('brhnqk,brhnke->brhnqe', p, vwin.astype(jnp.float32))

    def from_sub(x):
        tail = x.shape[5:]
        x = x.reshape((B, dil, Hg, Lp) + tail)[:, :, :, :L]
        perm = (0, 3, 1, 2) + tuple(range(4, 4 + len(tail)))
        return x.transpose(perm).reshape((B, T, Hg) + tail)

    return from_sub(acc), from_sub(m), from_sub(l)

def token_mixer(h, w_in, ret_log_decay_fwd, ret_log_decay_bwd, ret_norm, w_ret_out, w_att_out, w_out):
    B, T, _ = h.shape
    proj = h @ w_in
    cuts = [RQ, 2 * RQ, 2 * RQ + RV, 2 * RQ + 2 * RV,
            2 * RQ + 2 * RV + AQ, 2 * RQ + 2 * RV + 2 * AQ, 2 * RQ + 2 * RV + 3 * AQ]
    rq, rk, rv, rg, aq, ak, av, gate_logits = jnp.split(proj, cuts, axis=-1)

    ret_inv = 1.0 / (ROPE_THETA ** jnp.linspace(0.0, 1.0, RET_DK // 2, dtype=jnp.float32))
    q = rotate(rq.reshape(B, T, RET_HEADS, RET_DK), ret_inv).transpose(0, 2, 1, 3)
    k = (rotate(rk.reshape(B, T, RET_HEADS, RET_DK), ret_inv) * (RET_DK ** -0.5)).transpose(0, 2, 1, 3)
    v = rv.reshape(B, T, RET_HEADS, RET_DV).transpose(0, 2, 1, 3)
    fwd = retention_one_direction(q, k, v, ret_log_decay_fwd, True)
    bwd = retention_one_direction(q[:, :, ::-1], k[:, :, ::-1], v[:, :, ::-1], ret_log_decay_bwd, False)[:, :, ::-1]
    ret = (fwd + bwd).transpose(0, 2, 1, 3)
    r32 = ret.astype(jnp.float32)
    r32 = r32 * lax.rsqrt(jnp.mean(r32 * r32, axis=-1, keepdims=True) + EPS)
    ret_n = (r32 * ret_norm.reshape(RET_HEADS, RET_DV).astype(jnp.float32)).reshape(B, T, RV).astype(h.dtype)
    branch_a = (jax.nn.silu(rg) * ret_n) @ w_ret_out

    att_inv = ROPE_THETA ** (-jnp.arange(0, ATT_DH, 2, dtype=jnp.float32) / ATT_DH)
    qa = rotate(aq.reshape(B, T, ATT_HEADS, ATT_DH), att_inv) * (ATT_DH ** -0.5)
    ka = rotate(ak.reshape(B, T, ATT_HEADS, ATT_DH), att_inv)
    va = av.reshape(B, T, ATT_HEADS, ATT_DH)
    accs, ms, ls = [], [], []
    for g, (window, dil) in enumerate(ATT_GROUPS):
        sl = slice(g * ATT_HEADS_PER_GROUP, (g + 1) * ATT_HEADS_PER_GROUP)
        acc, m, l = dilated_group_attention(qa[:, :, sl], ka[:, :, sl], va[:, :, sl], window, dil)
        accs.append(acc); ms.append(m); ls.append(l)
    m_all = jnp.stack(ms)
    m_max = jnp.max(m_all, axis=0)
    w = jnp.exp(m_all - m_max[None])
    num = jnp.sum(w[..., None] * jnp.stack(accs), axis=0)
    den = jnp.sum(w * jnp.stack(ls), axis=0)
    att = (num / den[..., None]).reshape(B, T, A_OUT).astype(h.dtype)
    branch_b = att @ w_att_out

    gates = jax.nn.sigmoid(gate_logits.reshape(B, T, N_BRANCHES, D_MODEL))
    merged = gates[:, :, 0] * branch_a + gates[:, :, 1] * branch_b
    return merged @ w_out

def expert_choice_ffn(h, w_router, w_exp_gate, w_exp_up, w_exp_down):
    B, T, D = h.shape
    N = B * T
    tok = h.reshape(N, D)
    aff = jax.nn.softmax((tok @ w_router).astype(jnp.float32), axis=-1)
    cap = EC_CAPACITY_FACTOR * N // N_EXPERTS
    gate, idx = lax.top_k(aff.T, cap)
    xs = tok[idx]
    hid = jax.nn.silu(jnp.einsum('ecd,edf->ecf', xs, w_exp_gate)) * jnp.einsum('ecd,edf->ecf', xs, w_exp_up)
    out = jnp.einsum('ecf,efd->ecd', hid, w_exp_down) * gate[..., None].astype(h.dtype)
    y = jnp.zeros((N, D), out.dtype).at[idx.reshape(-1)].add(out.reshape(-1, D))
    return y.reshape(B, T, D).astype(h.dtype)

def encoder(x, norm_mix, w_in, ret_log_decay_fwd, ret_log_decay_bwd, ret_norm, w_ret_out, w_att_out, w_out,
            norm_ffn, w_router, w_exp_gate, w_exp_up, w_exp_down, norm_final):
    for layer in range(DEPTH):
        h = rmsnorm(x, norm_mix[layer])
        x = x + token_mixer(h, w_in[layer], ret_log_decay_fwd[layer], ret_log_decay_bwd[layer], ret_norm[layer],
                            w_ret_out[layer], w_att_out[layer], w_out[layer])
        h = rmsnorm(x, norm_ffn[layer])
        x = x + expert_choice_ffn(h, w_router[layer], w_exp_gate[layer], w_exp_up[layer], w_exp_down[layer])
    return rmsnorm(x, norm_final)

def setup_inputs(seed: int = 0) -> dict:
    key = jax.random.key(seed)
    ks = jax.random.split(key, 20)
    f32 = jnp.float32

    def nrm(k, shape, scale):
        return jax.random.normal(k, shape, f32) * scale

    base_decay = jnp.log(1.0 - 2.0 ** (-5.0 - jnp.arange(RET_HEADS, dtype=f32)))
    return {
        "x_prompt": nrm(ks[0], (BATCH, SEQ, D_MODEL), 1.0),
        "x_sample": nrm(ks[1], (DEC_BATCH, DEC_SEQ, D_MODEL), 1.0),
        "norm_mix": 1.0 + nrm(ks[2], (DEPTH, D_MODEL), 0.02),
        "w_in": nrm(ks[3], (DEPTH, D_MODEL, IN_COLS), D_MODEL ** -0.5),
        "ret_log_decay_fwd": base_decay[None] * jnp.exp(nrm(ks[4], (DEPTH, RET_HEADS), 0.1)),
        "ret_log_decay_bwd": base_decay[None] * jnp.exp(nrm(ks[5], (DEPTH, RET_HEADS), 0.1)),
        "ret_norm": 1.0 + nrm(ks[6], (DEPTH, RV), 0.02),
        "w_ret_out": nrm(ks[7], (DEPTH, RV, D_MODEL), RV ** -0.5),
        "w_att_out": nrm(ks[8], (DEPTH, A_OUT, D_MODEL), A_OUT ** -0.5),
        "w_out": nrm(ks[9], (DEPTH, D_MODEL, D_MODEL), D_MODEL ** -0.5),
        "norm_ffn": 1.0 + nrm(ks[10], (DEPTH, D_MODEL), 0.02),
        "w_router": nrm(ks[11], (DEPTH, D_MODEL, N_EXPERTS), D_MODEL ** -0.5),
        "w_exp_gate": nrm(ks[12], (DEPTH, N_EXPERTS, D_MODEL, EXPERT_HIDDEN), D_MODEL ** -0.5),
        "w_exp_up": nrm(ks[13], (DEPTH, N_EXPERTS, D_MODEL, EXPERT_HIDDEN), D_MODEL ** -0.5),
        "w_exp_down": nrm(ks[14], (DEPTH, N_EXPERTS, EXPERT_HIDDEN, D_MODEL), EXPERT_HIDDEN ** -0.5),
        "norm_final": 1.0 + nrm(ks[15], (D_MODEL,), 0.02),
    }

def reference(x_prompt, x_sample, norm_mix, w_in, ret_log_decay_fwd, ret_log_decay_bwd, ret_norm, w_ret_out,
              w_att_out, w_out, norm_ffn, w_router, w_exp_gate, w_exp_up, w_exp_down, norm_final):
    y_prompt = encoder(x_prompt, norm_mix, w_in, ret_log_decay_fwd, ret_log_decay_bwd, ret_norm, w_ret_out,
                       w_att_out, w_out, norm_ffn, w_router, w_exp_gate, w_exp_up, w_exp_down, norm_final)
    y_sample = encoder(x_sample, norm_mix, w_in, ret_log_decay_fwd, ret_log_decay_bwd, ret_norm, w_ret_out,
                       w_att_out, w_out, norm_ffn, w_router, w_exp_gate, w_exp_up, w_exp_down, norm_final)
    return (y_prompt, y_sample)


_drawn_inputs = setup_inputs


def setup_inputs(seed=0):
    import zlib

    import numpy as np

    out = dict(_drawn_inputs(seed))
    spreads = {}
    factors = {'norm_mix': 3.18, 'ret_norm': 4.974, 'norm_ffn': 3.349, 'norm_final': 2.857}
    for name, (base, spread) in spreads.items():
        noise = np.random.default_rng([zlib.crc32(name.encode()), seed]).standard_normal(out[name].shape)
        drawn = base * np.exp(spread * noise) if base else spread * noise
        out[name] = __import__('jax').numpy.asarray(drawn.astype(out[name].dtype))
    for name, factor in factors.items():
        out[name] = (out[name] * factor).astype(out[name].dtype)
    return out
```

```python
from contextlib import ExitStack, contextmanager

import numpy as np

import concourse.bass as bass
from concourse import mybir

F32 = mybir.dt.float32
F32R = mybir.dt.float32r
BF16 = mybir.dt.bfloat16
F16 = mybir.dt.float16
U32 = mybir.dt.uint32
ALU = mybir.AluOpType
ACT = mybir.ActivationFunctionType
AXX = mybir.AxisListType.X

P = 128
D = 1024
KC = D // P
T = 512
NB = 2
NT = T // P
RH, RDK, RDV = 4, 128, 256
NG, HG, DH = 3, 8, 64
HP = HG // 2
NE, FH = 16, 2048
CAP = 2 * T // NE
RES = 4
WIN0 = 64
EPS = 1e-6
MASKED = -1.0e30

NA, NBC, NC = 256, 384, 256
UNIT = KC * NBC
HEADS_LOOP = RH - 1

PIECES = ((0, 3), (3, 6), (6, 8))
PER_HEAD = {"w": 6, "piece": 18, "proj": 24, "tr": 34, "sc": 20, "out": 6, "turn": 16, "rope": 16, "ret": 1,
            "score": 8, "step": 8, "link": 11}
PER_COL = {"w": 4, "piece": 4, "proj": 16, "mix": 4}
PER_BATCH = {"w": 44, "piece": 94, "proj": 176, "tr": 164, "sc": 80, "out": 28, "turn": 64, "rope": 64, "ret": 4,
             "score": 32, "step": 32, "mix": 16, "f": 8, "hi": 28, "lo": 20, "link": 54}

MK = 2
MN = 1024
RAW_SLOTS, SPLIT_SLOTS = 8, 4
UNITS = NE * 24

START = 1


class Tally:

    def __init__(self, slots=1):
        self.slots, self.items, self.laps, self.k = slots, 0, 0, 0

    def n(self, more=0):
        return self.items + (self.k + more)

    @property
    def slot(self):
        return self.k % self.slots

    @property
    def lap(self):
        return self.laps + self.k // self.slots


@contextmanager
def rolled(eng, count, tallies, per):
    with eng.Fori(0, count) as i:
        kept = {}
        for name, t in tallies.items():
            step = per.get(name, 0)
            assert step % t.slots == 0, name
            kept[name] = (t.items, t.laps, t.k)
            if step:
                t.items = t.items + i * step
                t.laps = t.laps + i * (step // t.slots)
        yield i
        for name, t in tallies.items():
            items, laps, k = kept[name]
            assert t.k - k == per.get(name, 0), (name, t.k - k, per.get(name, 0))
            t.items, t.laps, t.k = items, laps, k + count * per.get(name, 0)


def head_schedule(att, proj):
    tiles = [(u, i) for u in (range(3) if proj else (3,)) for i in range(NT)]
    out, behind = [], []

    def project(n):
        for _ in range(n):
            if tiles:
                u, i = tiles.pop(0)
                out.append(("P", u, i))
                if i < len(PIECES):
                    out.append(("W", i))
                if behind:
                    out.append(behind.pop(0))
                if u == 0:
                    behind.append(("R", 0, i))

    steps = 2 * NT
    for s in range(steps + 1):
        if att and s == 0:
            project(1)
        if att and s < steps:
            out.append(("S", s))
        if proj or s % 3:
            project(1)
        if att and s == NT + 1:
            out.append(("V", 0))
        if att and s > 0:
            out.append(("T", s - 1))
        project(1 if proj and s % 3 == 0 and s > 0 else 0)
    project(12)
    out.extend(behind)
    if att:
        out.append(("V", 1))
    return out


def retention_schedule():
    extra = {1: ("K", 0), 2: ("K", 1), 3: ("K", 2), 4: ("K", 3), 5: ("O", 0), 6: ("O", 1), 7: ("O", 2),
             8: ("O", 3), 10: ("A", 0), 11: ("A", 1)}
    out, behind = [("G",)], []
    for n in range(NG * NT):
        g, i = divmod(n, NT)
        out.append(("P", g, i))
        if i < len(PIECES):
            out.append(("W", i))
        if n in extra:
            out.append(extra[n])
        if behind:
            out.append(behind.pop(0))
        behind.append(("R", g, i))
    out.extend(behind)
    return out


def hybrid_encoder(nc, x, w_a, w_b, w_c, w_ca, w_d, w_router, gains, decays, norm_final,
                   w_gate, w_up, w_down, ident_c, rope_r_c, rope_a_c, mask0_c, mask12_c, dist_c,
                   normed, y, out):
    ctx = ExitStack()
    with ctx:
        base = 16512
        cursor = [base]

        def put(name, shape, dt, at=None):
            size = int(np.prod(shape[1:])) * {F32: 4, F32R: 4, U32: 4, BF16: 2, F16: 2}[dt]
            size = -(-size // 32) * 32
            place = cursor[0] if at is None else at
            if at is None:
                cursor[0] += size
            return nc.alloc_sbuf_tensor_at(name, shape, dt, offset=place), place, size

        ident, _, _ = put("ident", [P, P], F32)
        rope_r, _, _ = put("rope_r", [P, NT, 2, RDK // 2], F32)
        rope_a, _, _ = put("rope_a", [P, RES, 2, DH // 2], F32)
        mask0, _, _ = put("mask0", [P, 7 * P], BF16)
        mask12, _, _ = put("mask12", [P, 2 * P], BF16)
        dist, _, _ = put("dist", [P, 2, 7 * P], F16)
        gain, _, _ = put("gain", [P, 3, KC], F32)
        decay_all, _, _ = put("decay_all", [P, RH, 2], F32)
        router, _, _ = put("router", [P, KC, NE], F32)
        small, small_at, _ = put("small", [P, 64], F32)
        aff_t, _, _ = put("aff_t", [NE, NB * T], F32)
        decay_cur = small[:, 0:2]
        ms = small[:, 4:8]
        rstd = small[:, 8:12]
        top = small[:, 12:16]
        psum_row = small[:, 16:18]
        pinv = small[:, 18:20]
        ret_ms = small[:, 20:24]
        ret_rstd = small[:, 24:28]
        soft = small[:, 28:32]
        soft_sum = small[:, 32:36]
        soft_inv = small[:, 36:40]
        shift = small[:, 40:42]
        ms_inv = small[:, 44:48]
        ret_inv = small[:, 48:52]
        y_ms = small[:, 52:60]
        y_inv = small[:, 4:12]

        h_hi, h_at, h_size = put("h_hi", [P, KC, T], F32R)
        h_lo, _, _ = put("h_lo", [P, KC, T], F32R)
        ret_t, ret_at, _ = put("ret_t", [P, KC, T], F32)
        att_t, att_at, _ = put("att_t", [P, HP, T], F32)
        w_at = cursor[0]
        w_raw = [put(f"w_raw{i}", [P, UNIT], F32)[0] for i in range(2)]
        w_hi = [put(f"w_hi{i}", [P, UNIT], F32R)[0] for i in range(2)]
        w_lo = [put(f"w_lo{i}", [P, UNIT], F32R)[0] for i in range(2)]
        xt, _, _ = put("xt", [P, NT, D], F32, at=ret_at)
        merged, _, _ = put("merged", [P, NT, D], F32, at=ret_at)

        area = cursor[0]
        decay, _, _ = put("decay", [P, 7 * P], F32)
        qk_t = [put(f"qk_t{g}", [P, 2, T], F32)[0] for g in range(NG)]
        v_a = [put(f"v_a{g}", [P, RES, P], F32)[0] for g in range(NG)]
        prob = [put(f"prob{i}", [P, 6 * P], F32)[0] for i in range(2)]
        prob_t, _, _ = put("prob_t", [P, RES + 2, T], F32)
        rqk_t, _, _ = put("rqk_t", [P, 2, T], F32)
        v_r, _, _ = put("v_r", [P, NT, RDV], F32)
        swish, _, _ = put("swish", [P, NT, RDV], F32)
        sd, _, _ = put("sd", [P, NT, T], F32)
        rot1 = [put(f"rot1_{i}", [P, 256], F32)[0] for i in range(2)]
        rot2 = [put(f"rot2_{i}", [P, 256], F32)[0] for i in range(2)]
        assert cursor[0] <= 229344, cursor[0]
        top_end = cursor[0]

        cursor[0] = area
        r_hi, _, _ = put("r_hi", [P, KC, T], F32R)
        r_lo, _, _ = put("r_lo", [P, KC, T], F32R)
        cursor[0] = area
        norm2, _, _ = put("norm2", [P, NT, D], F32)
        norm2_t, _, _ = put("norm2_t", [P, 2, KC, P], F32)
        aff, _, _ = put("aff", [P, NT, NE], F32)
        tmp = [put(f"tmp{i}", [P, T], F32)[0] for i in range(2)]
        aff_pad, _, _ = put("aff_pad", [48, T], F32)
        best, _, _ = put("best", [48, CAP], F32)
        best_at, _, _ = put("best_at", [48, CAP], U32)
        best_f, _, _ = put("best_f", [48, CAP], F32)
        assert cursor[0] <= area + 65536 
        cursor[0] = area + 32768
        a_hi, _, _ = put("a_hi", [P, HP, T], F32R)
        a_lo, _, _ = put("a_lo", [P, HP, T], F32R)
        gate_s = [put(f"gate_s{i}", [P, NT, NC], F32)[0] for i in range(2)]
        assert cursor[0] <= 229344

        cursor[0] = w_at
        m_raw = [put(f"m_raw{i}", [P, MK, MN], F32)[0] for i in range(RAW_SLOTS - 1)]
        y_tile, _, _ = put("y_tile", [P, NB * NT, D], F32, at=w_at)
        m_gate, _, _ = put("m_gate", [P, NE], F32)
        m_index, _, _ = put("m_index", [P, NE], U32)
        gate_now, _, _ = put("gate_now", [P, 8], F32)
        index_get, _, _ = put("index_get", [P, 8], U32)
        index_add, _, _ = put("index_add", [P, 8], U32)
        final_gain, _, _ = put("final_gain", [P, D], F32)
        assert cursor[0] <= area
        cursor[0] = h_at
        m_hi = [put(f"m_hi{i}", [P, MK, MN], F32R)[0] for i in range(SPLIT_SLOTS)]
        assert cursor[0] <= ret_at
        cursor[0] = ret_at
        hid_hi, _, _ = put("hid_hi", [P, KC, P], F32R)
        hid_lo, _, _ = put("hid_lo", [P, KC, P], F32R)
        m_raw.append(put(f"m_raw{RAW_SLOTS - 1}", [P, MK, MN], F32)[0])
        assert cursor[0] <= att_at
        cursor[0] = att_at
        m_lo = [put("m_lo0", [P, MK, MN], F32R)[0]]
        assert cursor[0] <= w_at
        cursor[0] = area + 36864
        m_lo += [put(f"m_lo{i}", [P, MK, MN], F32R)[0] for i in range(1, SPLIT_SLOTS)]
        assert cursor[0] <= 229344
        cursor[0] = area
        xs, _, _ = put("xs", [P, D], F32)
        xs_hi, _, _ = put("xs_hi", [P, KC, P], F32R)
        xs_lo, _, _ = put("xs_lo", [P, KC, P], F32R)
        m_swish, _, _ = put("m_swish", [P, MN], F32)
        hid, _, _ = put("hid", [P, MN], F32)
        scaled, _, _ = put("scaled", [P, D], F32)
        m_tmp = [put(f"m_tmp{i}", [P, T], F32)[0] for i in range(2)]
        assert cursor[0] <= area + 36864

        bank = [ctx.enter_context(nc.psum_tensor(f"bank{i}", [P, 2, 512], F32)) for i in range(4)]
        ps_proj, ps_tr, ps_sc, ps_out = bank
        ps_g, ps_t, ps_u, ps_d = bank

        def sem(name):
            return ctx.enter_context(nc.semaphore(name))

        s_const = sem("consts_loaded")
        s_x = [sem(f"x_loaded{i}") for i in range(NT)]
        s_xr = [sem(f"x_reloaded{i}") for i in range(NT)]
        s_wraw = [sem(f"weights_loaded{i}") for i in range(2)]
        s_whi = sem("weights_hi")
        s_wlo = [sem(f"weights_lo{i}") for i in range(2)]
        s_proj = sem("tile_projected")
        s_proj_free = [sem(f"projection_read{i}") for i in range(2)]
        s_tr = sem("transposed")
        s_tr_free = [sem(f"transposed_read{i}") for i in range(2)]
        s_sc = sem("scores_done")
        s_sc_free = [sem(f"scores_read{i}") for i in range(2)]
        s_out = sem("outputs_done")
        s_out_free = [sem(f"outputs_read{i}") for i in range(2)]
        s_gated = sem("outputs_gated")
        s_link = sem("vector_step_done")
        s_ms = sem("mean_square_ready")
        s_var = sem("inverse_variance_ready")
        s_rstd = sem("rstd_ready")
        s_xn = sem("tile_normalised")
        s_hi = sem("operand_hi")
        s_lo = sem("operand_lo")
        s_rope_x = sem("rotation_products")
        s_rope = sem("rotated")
        s_dexp = sem("decay_exponents")
        s_decay = sem("decays_ready")
        s_swish = sem("retention_gate_ready")
        s_rvar = sem("retention_inverse_variance")
        s_rrstd = sem("retention_rstd")
        s_rn = sem("retention_normalised")
        s_sm = sem("masked_scores")
        s_exp = sem("probabilities")
        s_prob = sem("probabilities_scaled")
        s_merged = sem("merged")
        s_gate = sem("first_gate_ready")
        s_n2 = sem("router_tile_normalised")
        s_shift = sem("router_shift")
        s_aff = sem("affinities")
        s_store_x = sem("mixed_tokens_stored")
        s_store_n = sem("normalised_tokens_stored")
        s_batch_stored = sem("batch_stored")
        s_best = sem("best_tokens")
        s_route = sem("routes_ready")
        s_mraw = [sem(f"expert_weights_loaded{i}") for i in range(RAW_SLOTS)]
        s_mhi = sem("expert_weights_hi")
        s_mlo = sem("expert_weights_lo")
        s_used = sem("expert_weights_used")
        s_mtr = sem("expert_transposed")
        s_mf = sem("expert_tokens_scaled")
        s_thi = sem("expert_operand_hi")
        s_tlo = sem("expert_operand_lo")
        s_sg = sem("expert_swish")
        s_hid = sem("expert_hidden")
        s_gnow = sem("expert_gate_picked")
        s_igot = sem("expert_index_picked")
        s_gather = sem("tokens_gathered")
        s_scaled = sem("expert_output_scaled")
        s_added = sem("expert_output_added")
        s_added_seen = sem("expert_output_add_seen")

        s_y = [sem(f"result_loaded{i}") for i in range(NB * NT)]
        s_ysq = sem("result_mean_square")
        s_yvar = sem("result_inverse_variance")
        s_yrstd = sem("result_rstd")
        s_yout = sem("result_normalised")
        s_stored = [sem(f"result_stored{i}") for i in range(2)]

        s_apart_sp, s_apart_dve, s_apart_pool = (sem(f"apart_{n}") for n in ("sync", "vector", "gpsimd"))

        n_const = 10
        primed = [*s_wlo, s_batch_stored, s_n2, s_proj, *s_tr_free, s_lo, *s_proj_free, s_out,
                  *s_out_free, *s_sc_free, s_sm, s_merged, s_scaled, s_added_seen]

        def apart(eng, spacer):
            eng.sem_inc(spacer, 1)

        def mixer_tallies():
            return {"w": Tally(2), "proj": Tally(2), "tr": Tally(2), "sc": Tally(2), "out": Tally(2),
                    "turn": Tally(2), "rope": Tally(2), "ret": Tally(), "score": Tally(2),
                    "step": Tally(2), "mix": Tally(), "f": Tally(2), "hi": Tally(), "lo": Tally(),
                    "link": Tally(), "piece": Tally()}

        def some(*names):
            return {k: v for k, v in mixer_tallies().items() if k in names}

        def all_read(eng, frees, t):
            eng.wait_ge(frees[0], START + t.lap + t.slot)
            eng.wait_ge(frees[1], START + t.lap)

        def residual_added(eng, proj, i):
            eng.wait_ge(s_proj_free[i % 2], START + proj.lap - 1 + i // 2)

        def thirds(a, groups):
            return a.rearrange("p (g h d) -> p g h d", g=groups, h=2)

        block = ctx.enter_context(nc.Block())

        @block.sync
        def _(sp):
            for dst, src in ((ident[:, :], ident_c), (rope_r[:, :, :, :], rope_r_c),
                             (rope_a[:, :, :, :], rope_a_c), (mask0[:, :], mask0_c),
                             (mask12[:, :], mask12_c), (dist[:, :, :], dist_c), (gain[:, :, :], gains),
                             (decay_all[:, :, :], decays), (router[:, :, :], w_router)):
                sp.dma_start(dst, src).then_inc(s_const, 16)
            t = {"w": Tally(2)}
            w = t["w"]

            def load_unit(src, size):
                sp.wait_ge(s_wlo[w.slot], START + w.lap)
                sp.dma_start(w_raw[w.slot][:, 0:size], src).then_inc(s_wraw[w.slot], 16)
                w.k += 1

            def load_head(h):
                for u in range(3):
                    load_unit(w_a[h, u], KC * NA)
                for u in range(3):
                    load_unit(w_b[h, u], KC * NBC)

            with rolled(sp, NB, t, PER_BATCH) as b:
                sp.wait_ge(s_batch_stored, START + b)
                sp.wait_ge(s_n2, START + b * NT)
                apart(sp, s_apart_sp)
                for i in range(NT):
                    sp.dma_start(xt[:, i, :], x[b, i]).then_inc(s_x[i], 16)
                load_head(0)
                with rolled(sp, HEADS_LOOP, t, {"w": 6}) as h:
                    load_head(h + 1)
                with rolled(sp, D // NC, t, {"w": 4}) as n:
                    for u in range(3):
                        load_unit(w_c[n, u], KC * NC)
                    load_unit(w_ca[n], HP * NC)
                for n in range(D // NC):
                    load_unit(w_d[n], KC * NC)
                    if n == 1:
                        sp.wait_ge(s_tr, b * PER_BATCH["tr"] + 152)
                        apart(sp, s_apart_sp)
                        for i in range(NT):
                            sp.dma_start(xt[:, i, :], x[b, i]).then_inc(s_xr[i], 16)
            sp.wait_ge(s_proj, START + NB * PER_BATCH["proj"])
            sp.dma_start(final_gain[:, :], norm_final).then_inc(s_const, 16)

            mt = {"raw": Tally(RAW_SLOTS), "unit": Tally()}

            def load_expert_unit(src):
                raw, unit = mt["raw"], mt["unit"]
                if unit.k == RAW_SLOTS - 1:
                    sp.wait_ge(s_store_x, 16 * NB * NT)
                    sp.wait_ge(s_n2, START + NB * NT)
                if unit.k >= RAW_SLOTS:
                    sp.wait_ge(s_mlo, unit.n(1 - RAW_SLOTS))
                    apart(sp, s_apart_sp)
                sp.dma_start(m_raw[raw.slot][:, :, :], src.rearrange("(c p) n -> p c n", p=P))\
                    .then_inc(s_mraw[raw.slot], 16)
                raw.k += 1
                unit.k += 1

            def load_in(weights, e, f):
                for j in range(4):
                    load_expert_unit(weights[e, MK * P * j:MK * P * (j + 1), MN * f:MN * (f + 1)])

            def load_down(e, f):
                for j in range(4):
                    row = MN * f + MK * P * j
                    load_expert_unit(w_down[e, row:row + MK * P, :])

            def load_expert(e, last):
                load_in(w_gate, e, 1)
                load_in(w_up, e, 1)
                load_down(e, 0)
                if not last:
                    load_in(w_gate, e + 1, 0)
                    load_in(w_up, e + 1, 0)
                load_down(e, 1)

            load_in(w_gate, 0, 0)
            load_in(w_up, 0, 0)
            with rolled(sp, NE - 1, mt, {"raw": 24, "unit": 24}) as e:
                load_expert(e, False)
            load_expert(NE - 1, True)

            sp.wait_ge(s_added, 16 * NE)
            sp.wait_ge(s_mlo, UNITS)
            for i in range(NB * NT):
                sp.dma_start(y_tile[:, i, :], y[P * i:P * (i + 1), :]).then_inc(s_y[i], 16)
            for i in range(NB * NT):
                sp.wait_ge(s_yout, i + 1)
                sp.dma_start(out[i // NT, i % NT], y_tile[:, i, :]).then_inc(s_stored[i % 2], 16)
            for i in range(2):
                sp.wait_ge(s_stored[i], 16 * NB * NT // 2)

        @block.gpsimd
        def _(pool):
            for each in primed:
                pool.sem_inc(each, START)
            t = some("turn", "mix", "proj")
            turn, mix, proj = t["turn"], t["mix"], t["proj"]

            def add_rotation():
                pool.wait_ge(s_rope_x, turn.n(1))
                pool.tensor_tensor(rot1[turn.slot][:, :], rot1[turn.slot][:, :], rot2[turn.slot][:, :],
                                   ALU.add).then_inc(s_rope, 1)
                turn.k += 1

            def add_rotations():
                for _ in range(NT + NG * NT):
                    add_rotation()
                proj.k += PER_HEAD["proj"]

            with rolled(pool, NB, t, PER_BATCH) as b:
                add_rotations()
                with rolled(pool, HEADS_LOOP, t, {"turn": 16, "proj": 24}):
                    add_rotations()
                pool.wait_ge(s_lo, START + b * PER_BATCH["lo"] + 20)
                apart(pool, s_apart_pool)
                with rolled(pool, D // NC, t, {"mix": 4, "proj": 16}) as n:
                    proj.k += 3 * NT
                    for i in range(NT):
                        pool.wait_ge(s_proj_free[proj.slot], START + proj.lap + 1)
                        pool.tensor_tensor(merged[:, i, bass.ds(n * NC, NC)], gate_s[0][:, i, :],
                                           gate_s[1][:, i, :], ALU.add).then_inc(s_merged, 1)
                        mix.k += 1
                        proj.k += 1
                proj.k += NT * (D // NC)
                for i in range(NT):
                    residual_added(pool, proj, i)
                    apart(pool, s_apart_pool)
                    pool.dma_start(y[bass.ds(b * T + i * P, P), :], xt[:, i, :]).then_inc(s_store_x, 16)
                for i in range(NT):
                    pool.wait_ge(s_n2, START + b * NT + i + 1)
                    apart(pool, s_apart_pool)
                    pool.dma_start(normed[bass.ds(b * T + i * P, P), :], norm2[:, i, :])\
                        .then_inc(s_store_n, 16)
                pool.wait_ge(s_store_x, b * (16 * NT) + 16 * NT)
                pool.wait_ge(s_store_n, b * (16 * NT) + 16 * NT)
                pool.sem_inc(s_batch_stored, 1)

            for i in range(SPLIT_SLOTS):
                pool.wait_ge(s_mhi, i + 1)
                pool.tensor_tensor(m_lo[i][:, :, :], m_raw[i][:, :, :], m_hi[i][:, :, :].bitcast(F32),
                                   ALU.subtract).then_inc(s_mlo, 1)

            pool.wait_ge(s_store_x, 16 * NB * NT)
            pool.wait_ge(s_route, 1)

            def gather(e, nth):
                pool.tensor_copy(index_get[:, 0:1], m_index[:, bass.ds(e, 1)]).then_inc(s_igot, 1)
                pool.wait_ge(s_igot, nth)
                apart(pool, s_apart_pool)
                pool.indirect_dma_start(
                    out=xs[:, :], out_offset=None, in_=normed,
                    in_offset=bass.IndirectOffsetOnAxis(ap=index_get[:, 0:1], axis=0)
                ).then_inc(s_gather, 16)

            def add(e, nth):
                pool.tensor_copy(index_add[:, 0:1], m_index[:, bass.ds(e, 1)]).then_inc(s_igot, 1)
                pool.wait_ge(s_igot, nth)
                pool.wait_ge(s_scaled, START + e + 1)
                apart(pool, s_apart_pool)
                pool.indirect_dma_start(
                    out=y, out_offset=bass.IndirectOffsetOnAxis(ap=index_add[:, 0:1], axis=0),
                    in_=scaled[:, :], in_offset=None, compute_op=ALU.add
                ).then_inc(s_added, 16)
                pool.wait_ge(s_added, e * 16 + 16)
                pool.sem_inc(s_added_seen, 1)

            gather(0, 1)
            pool.wait_ge(s_mtr, 2)
            pool.wait_ge(s_gather, 16)
            gather(1, 2)
            with pool.Fori(0, NE - 2) as e:
                pool.wait_ge(s_mtr, e * 6 + 6)
                pool.wait_ge(s_gather, e * 16 + 32)
                gather(e + 2, e * 2 + 3)
                add(e, e * 2 + 4)
            add(NE - 2, 2 * NE - 1)
            add(NE - 1, 2 * NE)

        @block.tensor
        def _(pe):
            t = some("w", "proj", "tr", "sc", "out", "rope", "ret", "step")
            w, proj, tr, sc, outs = t["w"], t["proj"], t["tr"], t["sc"], t["out"]

            def project(cols, chunks, hi, lo, tokens):
                sl = w.slot
                wh = w_hi[sl][:, 0:chunks * cols].rearrange("p (c n) -> p c n", c=chunks)
                wl = w_lo[sl][:, 0:chunks * cols].rearrange("p (c n) -> p c n", c=chunks)
                pe.wait_ge(s_proj_free[proj.slot], START + proj.lap)
                for c in range(chunks):
                    for n, (a, v) in enumerate(((hi, wh), (hi, wl), (lo, wh))):
                        last = pe.matmul(ps_proj[:, proj.slot, 0:cols], a[:, c, tokens], v[:, c, :],
                                         start=c == n == 0, stop=c == chunks - 1 and n == 2)
                last.then_inc(s_proj, 1)
                proj.k += 1

            def unit_ready():
                pe.wait_ge(s_wlo[w.slot], START + w.lap + 1)

            def transposes(ins, rows=P, cols=P):
                pe.wait_ge(s_tr_free[tr.slot], START + tr.lap)
                for j, a in enumerate(ins):
                    last = pe.transpose(ps_tr[0:cols, tr.slot, rows * j:rows * (j + 1)], a,
                                        ident[0:rows, 0:rows])
                last.then_inc(s_tr, 1)
                tr.k += 1

            def natural(i):
                return slice(i * P, (i + 1) * P)

            def residue(i):
                return slice(i, T, RES)

            def run(schedule, kind):
                rope, step = t["rope"], t["step"]
                earlier = proj.lap + proj.slot, proj.lap
                for what, *arg in schedule:
                    if what == "P":
                        u, i = arg
                        if i == 0:
                            unit_ready()
                        if kind == "head":
                            project(NA, KC, h_hi, h_lo, natural(i))
                        else:
                            project(NBC, KC, h_hi, h_lo, residue(i))
                        if i == NT - 1:
                            w.k += 1
                    elif what == "R":
                        pe.wait_ge(s_rope, rope.n(1))
                        transposes([rot1[rope.slot][:, 0:P], rot1[rope.slot][:, P:2 * P]])
                        rope.k += 1
                    elif what == "S":
                        s = arg[0]
                        a, r = divmod(s, RES)
                        rows = slice(DH * a, DH * (a + 1))
                        if s == 0:
                            all_read(pe, s_tr_free, tr)
                        q = [qk_t[g][rows, 0, natural(r)] for g in range(NG)]
                        pe.wait_ge(s_sc_free[sc.slot], START + sc.lap)
                        pe.matmul(ps_sc[:, sc.slot, :], q[0], qk_t[0][rows, 1, :],
                                  start=True, stop=True).then_inc(s_sc, 1)
                        sc.k += 1
                        pe.wait_ge(s_sc_free[sc.slot], START + sc.lap)
                        for g in (1, 2):
                            last = pe.matmul(ps_sc[:, sc.slot, P * (g - 1):P * g], q[g],
                                             qk_t[g][rows, 1, natural(r)], start=True, stop=True)
                        last.then_inc(s_sc, 1)
                        sc.k += 1
                    elif what == "T":
                        pe.wait_ge(s_prob, step.n(1))
                        p = prob[step.slot]
                        transposes([p[:, natural(j)] for j in range(4)])
                        transposes([p[:, natural(j)] for j in range(4, 6)])
                        step.k += 1
                    elif what == "V":
                        a = arg[0]
                        rows = slice(DH * a, DH * (a + 1))
                        all_read(pe, s_tr_free, tr)
                        if a == 0:
                            pe.wait_ge(s_proj_free[0], START + earlier[0])
                            pe.wait_ge(s_proj_free[1], START + earlier[1])
                        pe.wait_ge(s_out_free[outs.slot], START + outs.lap)
                        for r in range(RES):
                            pe.matmul(ps_out[rows, outs.slot, :], v_a[0][:, r, rows], prob_t[:, r, :],
                                      start=r == 0, stop=False)
                        for g in (1, 2):
                            for r in range(RES):
                                last = pe.matmul(ps_out[rows, outs.slot, natural(r)], v_a[g][:, r, rows],
                                                 prob_t[:, RES + g - 1, natural(r)],
                                                 start=False, stop=g == 2 and r == RES - 1)
                        last.then_inc(s_out, 1)
                        outs.k += 1
                    elif what == "K":
                        j = arg[0]
                        if j == 0:
                            all_read(pe, s_tr_free, tr)
                            pe.wait_ge(s_swish, t["ret"].n(1))
                        pe.wait_ge(s_sc_free[sc.slot], START + sc.lap)
                        pe.matmul(ps_sc[:, sc.slot, :], rqk_t[:, 1, natural(j)], rqk_t[:, 0, :],
                                  start=True, stop=True).then_inc(s_sc, 1)
                        sc.k += 1
                    elif what == "O":
                        i = arg[0]
                        if i == 0:
                            all_read(pe, s_sc_free, sc)
                        pe.wait_ge(s_out_free[outs.slot], START + outs.lap)
                        for j in range(NT):
                            last = pe.matmul(ps_out[:, outs.slot, 0:RDV], sd[:, j, natural(i)], v_r[:, j, :],
                                             start=j == 0, stop=j == NT - 1)
                        last.then_inc(s_out, 1)
                        outs.k += 1
                    elif what == "A":
                        c = arg[0]
                        pe.wait_ge(s_rn, t["ret"].n(1))
                        transposes([swish[:, i, natural(c)] for i in range(NT)])
                        if c == 1:
                            t["ret"].k += 1

            pe.wait_ge(s_const, 16 * (n_const - 1))
            with rolled(pe, NB, t, PER_BATCH) as b:
                for i in range(NT):
                    pe.wait_ge(s_xn, b * NT + i + 1)
                    for half in range(2):
                        transposes([xt[:, i, natural(4 * half + j)] for j in range(4)])
                pe.wait_ge(s_lo, START + b * PER_BATCH["lo"] + 8)

                run(head_schedule(False, True), "head")
                run(retention_schedule(), "att")
                with rolled(pe, HEADS_LOOP, t, PER_HEAD):
                    run(head_schedule(True, True), "head")
                    run(retention_schedule(), "att")
                run(head_schedule(True, False), "head")

                def columns(last):
                    for u in (1, 2, 3) if last else (1, 2, 3, 0):
                        unit_ready()
                        if u == 2:
                            pe.wait_ge(s_lo, START + b * PER_BATCH["lo"] + 20)
                        for i in range(NT):
                            if u < 3:
                                a, l = ((h_hi, h_lo), (h_hi, h_lo), (r_hi, r_lo))[u]
                                project(NC, KC, a, l, natural(i))
                            else:
                                project(NC, HP, a_hi, a_lo, natural(i))
                        w.k += 1

                with rolled(pe, D // NC - 1, t, PER_COL):
                    columns(False)
                columns(True)

                pe.wait_ge(s_merged, START + b * PER_BATCH["mix"] + 16)
                for i in range(NT):
                    for half in range(2):
                        transposes([merged[:, i, natural(4 * half + j)] for j in range(4)])
                all_read(pe, s_tr_free, tr)
                for n in range(D // NC):
                    unit_ready()
                    for i in range(NT):
                        project(NC, KC, h_hi, h_lo, natural(i))
                    w.k += 1

                for i in range(NT):
                    pe.wait_ge(s_n2, START + b * NT + i + 1)
                    for half in range(2):
                        transposes([norm2[:, i, natural(4 * half + j)] for j in range(4)])
                    all_read(pe, s_tr_free, tr)
                    pe.wait_ge(s_out_free[outs.slot], START + outs.lap)
                    for c in range(KC):
                        last = pe.matmul(ps_out[:, outs.slot, 0:NE], norm2_t[:, i % 2, c, :], router[:, c, :],
                                         start=c == 0, stop=c == KC - 1)
                    last.then_inc(s_out, 1)
                    outs.k += 1
                for i in range(NT):
                    pe.wait_ge(s_aff, b * NT + i + 1)
                    transposes([aff[:, i, :]], cols=NE)

            for n, a in enumerate((best, best_f)):
                pe.wait_ge(s_best, 1)
                pe.wait_ge(s_tr_free[tr.slot], START + tr.lap)
                pe.transpose(ps_tr[0:CAP, tr.slot, 0:48], a[:, :], ident[0:48, 0:48]).then_inc(s_tr, 1)
                tr.k += 1
            pe.wait_ge(s_route, 1)

            mt = {"unit": Tally(), "slot": Tally(SPLIT_SLOTS), "tr": Tally(), "step": Tally(), "op": Tally()}
            unit, slot, mtr, step, op = mt["unit"], mt["slot"], mt["tr"], mt["step"], mt["op"]

            def use(ps, hi, lo, chunk, first, last):
                pe.wait_ge(s_mlo, unit.n(1))
                wh, wl = m_hi[slot.slot], m_lo[slot.slot]
                for k in range(MK):
                    for n, (a, v) in enumerate(((hi, wh), (hi, wl), (lo, wh))):
                        for half in range(2):
                            mm = pe.matmul(ps[:, half, :], a[:, chunk + k, :],
                                           v[:, k, 512 * half:512 * (half + 1)],
                                           start=first and k == n == 0,
                                           stop=last and k == MK - 1 and n == 2)
                mm.then_inc(s_used, 1)
                unit.k += 1
                slot.k += 1

            def gate_cols():
                pe.wait_ge(s_sg, step.n())
                for j in range(4):
                    use(ps_g, xs_hi, xs_lo, MK * j, j == 0, j == 3)

            def up_cols():
                pe.wait_ge(s_hid, step.n())
                for j in range(4):
                    use(ps_u, xs_hi, xs_lo, MK * j, j == 0, j == 3)
                step.k += 1

            def expert_transposes(ins):
                for half in range(2):
                    if mtr.k >= 2:
                        pe.wait_ge(s_tlo, mtr.n(-1))
                    for j in range(4):
                        last = pe.transpose(ps_t[:, half, natural(j)], ins[:, natural(4 * half + j)],
                                            ident[:, :])
                    last.then_inc(s_mtr, 1)
                    mtr.k += 1

            def hidden_transposes(nth):
                pe.wait_ge(s_hid, nth)
                expert_transposes(hid)

            def token_transposes(nth):
                pe.wait_ge(s_gather, nth)
                expert_transposes(xs)

            def operand_ready(later=0):
                pe.wait_ge(s_tlo, mtr.n(-later))

            def down(e, f, later=0):
                operand_ready(later)
                if f == 0:
                    pe.wait_ge(s_scaled, START + e)
                for j in range(4):
                    use(ps_d, hid_hi, hid_lo, MK * j, f == 0 and j == 0, f == 1 and j == 3)

            def expert(e, last):
                gate_cols()
                hidden_transposes(e * 2 + 1)
                up_cols()
                if not last:
                    token_transposes(e * 16 + 32)
                down(e, 0, 0 if last else 2)
                if not last:
                    operand_ready()
                    gate_cols()
                hidden_transposes(e * 2 + 2)
                if not last:
                    up_cols()
                down(e, 1)

            token_transposes(16)
            operand_ready()
            gate_cols()
            up_cols()
            with rolled(pe, NE - 1, mt, {"unit": 24, "slot": 24, "tr": 6, "step": 2}) as e:
                expert(e, False)
            expert(NE - 1, True)

        @block.scalar
        def _(act):
            t = some("w", "proj", "tr", "sc", "out", "turn", "ret", "score", "mix", "hi")
            w, proj, tr, outs = t["w"], t["proj"], t["tr"], t["out"]

            def split_unit(size, part=None):
                lo, hi = (0, 8) if part is None else PIECES[part]
                cols = slice(size // 8 * lo, size // 8 * hi)
                act.wait_ge(s_wraw[w.slot], w.lap * 16 + 16)
                act.wait_ge(s_proj, START + w.items * NT + (NT * (w.k - 1) if w.k >= 2 else 0))
                act.activation(w_hi[w.slot][:, cols], w_raw[w.slot][:, cols], ACT.Copy)\
                    .then_inc(s_whi, 1)
                if hi == 8:
                    w.k += 1

            def operand_hi(dst, src, scale=1.0):
                act.activation(dst, src, ACT.Copy, scale=scale).then_inc(s_hi, 1)
                t["hi"].k += 1

            def run(schedule, kind, sizes):
                ret, score = t["ret"], t["score"]
                sizes = list(sizes)
                for what, *arg in schedule:
                    if what == "W":
                        split_unit(sizes[0], arg[0])
                        if arg[0] == len(PIECES) - 1:
                            sizes.pop(0)
                    elif what == "P" and arg[0] == 3:
                        i = arg[1]
                        if i == 0:
                            act.wait_ge(s_tr, tr.n())
                        act.wait_ge(s_proj, START + proj.n(1))
                        act.activation(gate_s[0][:, i, :], ps_proj[:, proj.slot, 0:NC], ACT.Copy)\
                            .then_inc(s_proj_free[proj.slot], 1)
                        proj.k += 1
                    elif what == "P" and kind == "head":
                        u, i = arg
                        if u > 0:
                            if (u, i) == (1, 0):
                                act.wait_ge(s_tr, tr.n())
                            act.wait_ge(s_proj, START + proj.n(1))
                            dst = v_r if u == 1 else swish
                            act.activation(dst[:, i, :], ps_proj[:, proj.slot, 0:NA], ACT.Copy)\
                                .then_inc(s_proj_free[proj.slot], 1)
                        else:
                            t["turn"].k += 1
                        proj.k += 1
                    elif what == "P":
                        g, i = arg
                        t["turn"].k += 1
                        if (g, i) == (0, 0):
                            act.wait_ge(s_out, START + outs.n())
                        act.wait_ge(s_rope_x, t["turn"].n())
                        act.activation(v_a[g][:, i, :], ps_proj[:, proj.slot, 2 * P:3 * P], ACT.Copy)\
                            .then_inc(s_proj_free[proj.slot], 1)
                        proj.k += 1
                    elif what == "R":
                        u, i = arg
                        act.wait_ge(s_tr, tr.n(1))
                        dst = rqk_t if kind == "head" else qk_t[u]
                        act.activation(dst[:, :, P * i:P * (i + 1)],
                                       ps_tr[:, tr.slot, 0:2 * P].rearrange("p (a n) -> p a n", a=2),
                                       ACT.Copy).then_inc(s_tr_free[tr.slot], 1)
                        tr.k += 1
                    elif what == "S":
                        i = score.slot
                        act.wait_ge(s_sm, START + score.n(1))
                        act.activation(prob[i][:, :], prob[i][:, :], ACT.Exp, bias=shift[:, i:i + 1],
                                       scale=DH ** -0.5, accum_out=psum_row[:, i:i + 1]).then_inc(s_exp, 1)
                        score.k += 1
                        t["sc"].k += 2
                    elif what == "T":
                        r = arg[0] % RES
                        if r == 0:
                            act.wait_ge(s_out, START + outs.n())
                        act.wait_ge(s_tr, tr.n(1))
                        act.activation(prob_t[:, 0:RES, P * r:P * (r + 1)],
                                       ps_tr[:, tr.slot, :].rearrange("p (a n) -> p a n", a=RES),
                                       ACT.Copy).then_inc(s_tr_free[tr.slot], 1)
                        tr.k += 2
                    elif what == "V":
                        outs.k += 1
                    elif what == "G":
                        act.wait_ge(s_dexp, ret.n(1))
                        act.activation(decay[:, :], decay[:, :], ACT.Exp).then_inc(s_decay, 1)
                        all_read(act, s_proj_free, proj)
                        act.activation(swish[:, :, :], swish[:, :, :], ACT.Silu).then_inc(s_swish, 1)
                    elif what == "K":
                        t["sc"].k += 1
                    elif what == "O":
                        i = arg[0]
                        act.wait_ge(s_gated, ret.n() * NT + (i + 1))
                        act.activation(ps_out[:, outs.slot, 0:RDV], ps_out[:, outs.slot, 0:RDV], ACT.Square,
                                       accum_out=ret_ms[:, i:i + 1]).then_inc(s_out_free[outs.slot], 1)
                        outs.k += 1
                        if i == NT - 1:
                            act.wait_ge(s_rvar, ret.n(1))
                            act.activation(ret_rstd, ret_inv, ACT.Sqrt).then_inc(s_rrstd, 1)
                    elif what == "A":
                        tr.k += 1
                        if arg[0] == 1:
                            ret.k += 1
                assert not sizes

            act.wait_ge(s_const, 16 * (n_const - 1))
            with rolled(act, NB, t, PER_BATCH) as b:
                act.wait_ge(s_batch_stored, START + b)
                for i in range(NT):
                    act.wait_ge(s_x[i], b * 16 + 16)
                    act.activation(norm2[:, i, :], xt[:, i, :], ACT.Square, accum_out=ms[:, i:i + 1])\
                        .then_inc(s_ms, 1)
                split_unit(KC * NA)
                act.wait_ge(s_var, b * 2 + 1)
                act.activation(rstd, ms_inv, ACT.Sqrt).then_inc(s_rstd, 1)
                for i in range(NT):
                    for half in range(2):
                        act.wait_ge(s_tr_free[tr.slot], START + tr.lap + 1)
                        operand_hi(h_hi[:, 4 * half:4 * half + 4, P * i:P * (i + 1)],
                                   tmp[tr.slot][:, :].rearrange("p (c n) -> p c n", c=4))
                        tr.k += 1

                a, bb = KC * NA, KC * NBC
                run(head_schedule(False, True), "head", (a, a, bb))
                run(retention_schedule(), "att", (bb, bb, a))
                with rolled(act, HEADS_LOOP, t, PER_HEAD):
                    run(head_schedule(True, True), "head", (a, a, bb))
                    run(retention_schedule(), "att", (bb, bb, a))
                run(head_schedule(True, False), "head", (a,))

                act.wait_ge(s_out, START + outs.n())
                all_read(act, s_out_free, outs)
                all_read(act, s_tr_free, tr)
                all_read(act, s_proj_free, proj)
                act.activation(gate_s[0][:, :, :], gate_s[0][:, :, :], ACT.Sigmoid).then_inc(s_gate, 1)

                def outputs_hi(chunks):
                    for c in chunks:
                        if c < KC:
                            operand_hi(r_hi[:, c, :], ret_t[:, c, :], gain[:, 2, c:c + 1])
                        else:
                            operand_hi(a_hi[:, c - KC, :], att_t[:, c - KC, :])

                def gate(u, i):
                    act.wait_ge(s_proj, START + proj.n(1))
                    act.activation(gate_s[u][:, i, :], ps_proj[:, proj.slot, 0:NC], ACT.Sigmoid)\
                        .then_inc(s_proj_free[proj.slot], 1)

                def columns(first, last):
                    for i in range(NT):
                        if not first:
                            act.wait_ge(s_merged, START + t["mix"].n(i + 1 - NT))
                        gate(1, i)
                        proj.k += 1
                        if i == 1:
                            split_unit(KC * NC)
                        if first:
                            outputs_hi(range(3 * i, 3 * i + 3))
                    for u in (2, 3):
                        for i in range(NT):
                            proj.k += 1
                            if i == 1:
                                split_unit((HP if u == 2 else KC) * NC)
                    if not last:
                        for i in range(NT):
                            act.wait_ge(s_merged, START + t["mix"].n(i + 1))
                            gate(0, i)
                            proj.k += 1
                            if i == 1:
                                split_unit(KC * NC)
                    t["mix"].k += NT

                columns(True, False)
                with rolled(act, D // NC - 2, t, PER_COL):
                    columns(False, False)
                columns(False, True)

                for i in range(NT):
                    for half in range(2):
                        act.wait_ge(s_tr, tr.n(1))
                        operand_hi(h_hi[:, 4 * half:4 * half + 4, P * i:P * (i + 1)],
                                   ps_tr[:, tr.slot, :].rearrange("p (c n) -> p c n", c=4))
                        tr.k += 1
                for n in range(D // NC):
                    for i in range(NT):
                        proj.k += 1
                        if i == 1 and n < D // NC - 1:
                            split_unit(KC * NC)

                for i in range(NT):
                    residual_added(act, proj, i)
                    act.activation(norm2[:, i, :], xt[:, i, :], ACT.Square, accum_out=ms[:, i:i + 1])\
                        .then_inc(s_ms, 1)
                act.wait_ge(s_var, b * 2 + 2)
                act.activation(rstd, ms_inv, ACT.Sqrt).then_inc(s_rstd, 1)
                for i in range(NT):
                    act.wait_ge(s_shift, b * NT + i + 1)
                    act.activation(aff[:, i, :], ps_out[:, outs.slot, 0:NE], ACT.Exp, bias=soft[:, i:i + 1],
                                   accum_out=soft_sum[:, i:i + 1]).then_inc(s_out_free[outs.slot], 1)
                    outs.k += 1
                tr.k += 3 * NT

            mt = {"raw": Tally(RAW_SLOTS), "slot": Tally(SPLIT_SLOTS), "unit": Tally(), "done": Tally(),
                  "tr": Tally(), "step": Tally()}
            raw, slot, unit, done, mtr, step = mt.values()

            def split_units(n=4):
                for _ in range(n):
                    act.wait_ge(s_mraw[raw.slot], raw.lap * 16 + 16)
                    if unit.k >= SPLIT_SLOTS:
                        act.wait_ge(s_used, unit.n(1 - SPLIT_SLOTS))
                    act.activation(m_hi[slot.slot][:, :, :], m_raw[raw.slot][:, :, :], ACT.Copy)\
                        .then_inc(s_mhi, 1)
                    for x in (raw, slot, unit):
                        x.k += 1

            def swish_step():
                act.wait_ge(s_used, done.n())
                act.wait_ge(s_hid, step.n())
                act.activation(m_swish[:, :], ps_g[:, :, :], ACT.Silu).then_inc(s_sg, 1)
                step.k += 1

            def hidden_hi():
                for half in range(2):
                    act.wait_ge(s_mtr, mtr.n(1))
                    act.activation(hid_hi[:, 4 * half:4 * half + 4, :], ps_t[:, half, :], ACT.Copy)\
                        .then_inc(s_thi, 1)
                    mtr.k += 1

            def tokens_hi(nth):
                for half in range(2):
                    act.wait_ge(s_mf, nth + half)
                    act.activation(xs_hi[:, 4 * half:4 * half + 4, :], m_tmp[half][:, :], ACT.Copy)\
                        .then_inc(s_thi, 1)
                    mtr.k += 1

            def after(units=4):
                done.k += units

            def expert(e, last):
                after()
                split_units()
                swish_step()
                hidden_hi()
                after()
                split_units()
                if not last:
                    tokens_hi(e * 2 + 3)
                after()
                split_units(2 if last else 4)
                if not last:
                    after()
                    split_units()
                    swish_step()
                hidden_hi()
                if last:
                    split_units(2)
                if not last:
                    after()
                    split_units()
                after()
                if not last:
                    split_units()
                act.activation(gate_now[:, 0:1], m_gate[:, bass.ds(e, 1)], ACT.Copy).then_inc(s_gnow, 1)
                act.wait_ge(s_gnow, e + 1)
                act.wait_ge(s_used, done.n())
                act.wait_ge(s_added_seen, START + e)
                act.activation(scaled[:, :], ps_d[:, :, :], ACT.Copy, scale=gate_now[:, 0:1])\
                    .then_inc(s_scaled, 1)

            split_units()
            act.wait_ge(s_route, 1)
            tokens_hi(1)
            after()
            split_units()
            swish_step()
            after()
            split_units()
            per = {"raw": 24, "slot": 24, "unit": 24, "done": 24, "tr": 6, "step": 2}
            with rolled(act, NE - 1, mt, per) as e:
                expert(e, False)
            expert(NE - 1, True)

            for i in range(NB * NT):
                act.wait_ge(s_y[i], 16)
                if i > 0:
                    act.wait_ge(s_ysq, i)
                act.activation(scaled[:, :], y_tile[:, i, :], ACT.Square, accum_out=y_ms[:, i:i + 1])\
                    .then_inc(s_ysq, 1)
                if i % 2 == 1:
                    act.wait_ge(s_yvar, (i + 1) // 2)
                    act.activation(y_ms[:, i - 1:i + 1], y_inv[:, i - 1:i + 1], ACT.Sqrt)\
                        .then_inc(s_yrstd, 1)

        @block.vector
        def _(dve):
            t = some("w", "piece", "proj", "tr", "sc", "out", "turn", "ret", "score", "step", "f", "hi", "lo",
                     "link")
            w, proj, tr, sc, outs, link = t["w"], t["proj"], t["tr"], t["sc"], t["out"], t["link"]

            def then(ins):
                ins.then_inc(s_link, 1)
                link.k += 1
                dve.wait_ge(s_link, link.n())

            def split_unit(size, part=None):
                lo, hi = (0, 8) if part is None else PIECES[part]
                cols = slice(size // 8 * lo, size // 8 * hi)
                dve.wait_ge(s_whi, t["piece"].n(1))
                ins = dve.tensor_tensor(w_lo[w.slot][:, cols], w_raw[w.slot][:, cols],
                                        w_hi[w.slot][:, cols].bitcast(F32), ALU.subtract)
                t["piece"].k += 1
                if hi == 8:
                    ins.then_inc(s_wlo[w.slot], 1)
                    w.k += 1

            def inverse(dst, src, width):
                then(dve.tensor_scalar(dst, src, 1.0 / width, EPS, ALU.mult, ALU.add))
                return dve.reciprocal(dst, dst)

            def rotate(table, i, groups):
                turn, half = t["turn"], 128 // groups
                dve.wait_ge(s_tr, tr.n())
                dve.wait_ge(s_proj, START + proj.n(1))
                q = ps_proj[:, proj.slot, 0:256]
                wide = q.rearrange("p (g d) -> p g d", d=half)
                a = rot1[turn.slot][:, :].rearrange("p (g d) -> p g d", d=half)
                dve.tensor_tensor(a, wide, table[:, i, 0, :].unsqueeze(1).to_broadcast([P, 2 * groups, half]),
                                  ALU.mult)
                x, y2 = thirds(q, groups), thirds(rot2[turn.slot][:, :], groups)
                sin = table[:, i, 1, :].unsqueeze(1).to_broadcast([P, groups, half])
                dve.scalar_tensor_tensor(y2[:, :, 0, :], x[:, :, 1, :], -1.0, sin, ALU.mult, ALU.mult)
                dve.tensor_tensor(y2[:, :, 1, :], x[:, :, 0, :], sin, ALU.mult).then_inc(s_rope_x, 1)
                turn.k += 1

            def scale_step():
                i = t["step"].slot
                dve.wait_ge(s_exp, t["step"].n(1))
                then(dve.reciprocal(pinv[:, i:i + 1], psum_row[:, i:i + 1]))
                dve.tensor_scalar(prob[i][:, :], prob[i][:, :], pinv[:, i:i + 1], None, ALU.mult)\
                    .then_inc(s_prob, 1)
                t["step"].k += 1

            def run(schedule, kind, sizes, att_head, ret_head):
                ret, score = t["ret"], t["score"]
                sizes = list(sizes)
                for what, *arg in schedule:
                    if what == "W":
                        split_unit(sizes[0], arg[0])
                        if arg[0] == len(PIECES) - 1:
                            sizes.pop(0)
                    elif what == "P" and arg[0] == 3:
                        proj.k += 1
                    elif what == "P" and kind == "head":
                        u, i = arg
                        if u == 0:
                            rotate(rope_r, i, 2)
                            dve.wait_ge(s_rope_x, t["turn"].n())
                            dve.sem_inc(s_proj_free[proj.slot], 1)
                        proj.k += 1
                    elif what == "P":
                        rotate(rope_a, arg[1], 4)
                        proj.k += 1
                    elif what == "R":
                        tr.k += 1
                    elif what == "S":
                        i, r = score.slot, arg[0] % RES
                        dve.wait_ge(s_tr, tr.n())
                        dve.wait_ge(s_sm, START + score.n())
                        dve.wait_ge(s_sc, sc.n(1))
                        apart(dve, s_apart_dve)
                        dve.tensor_tensor_reduce(
                            out=prob[i][:, 0:T], in0=ps_sc[:, sc.slot, :],
                            in1=mask0[:, P * (3 - r):P * (3 - r) + T], scale=1.0, scalar=-3.0e38,
                            op0=ALU.add, op1=ALU.max, accum_out=top[:, 0:1]).then_inc(s_sc_free[sc.slot], 1)
                        sc.k += 1
                        dve.wait_ge(s_sc, sc.n(1))
                        apart(dve, s_apart_dve)
                        dve.tensor_tensor_reduce(
                            out=prob[i][:, T:T + 2 * P], in0=ps_sc[:, sc.slot, 0:2 * P],
                            in1=mask12[:, :], scale=1.0, scalar=-3.0e38,
                            op0=ALU.add, op1=ALU.max, accum_out=top[:, 1:2]).then_inc(s_sc_free[sc.slot], 1)
                        sc.k += 1
                        all_read(dve, s_sc_free, sc)
                        dve.tensor_scalar(shift[:, i:i + 1], top[:, 0:1], top[:, 1:2], -DH ** -0.5,
                                          ALU.max, ALU.mult).then_inc(s_sm, 1)
                        score.k += 1
                        if arg[0] > 0:
                            scale_step()
                    elif what == "T":
                        s = arg[0]
                        r = s % RES
                        if s == 2 * NT - 1:
                            scale_step()
                        if r == 0:
                            dve.wait_ge(s_out, START + outs.n())
                        tr.k += 1
                        dve.wait_ge(s_tr, tr.n(1))
                        dve.tensor_copy(prob_t[:, RES:RES + 2, P * r:P * (r + 1)],
                                        ps_tr[:, tr.slot, 0:2 * P].rearrange("p (a n) -> p a n", a=2))\
                            .then_inc(s_tr_free[tr.slot], 1)
                        tr.k += 1
                    elif what == "V":
                        rows = slice(DH * arg[0], DH * (arg[0] + 1))
                        dve.wait_ge(s_out, START + outs.n(1))
                        dve.tensor_copy(att_t[rows, att_head, :].rearrange("p (t r) -> p r t", r=RES),
                                        ps_out[rows, outs.slot, :].rearrange("p (r t) -> p r t", r=RES))\
                            .then_inc(s_out_free[outs.slot], 1)
                        outs.k += 1
                    elif what == "G":
                        all_read(dve, s_sc_free, sc)
                        then(dve.tensor_copy(decay_cur, decay_all[:, ret_head, :]))
                        then(dve.tensor_scalar(decay[:, :], dist[:, 1, :], decay_cur[:, 1:2], None, ALU.mult))
                        dve.scalar_tensor_tensor(decay[:, :], dist[:, 0, :], decay_cur[:, 0:1], decay[:, :],
                                                 ALU.mult, ALU.add).then_inc(s_dexp, 1)
                    elif what == "K":
                        j = arg[0]
                        if j == 0:
                            dve.wait_ge(s_decay, ret.n(1))
                        dve.wait_ge(s_sc, sc.n(1))
                        at = P * (NT - 1 - j)
                        dve.scalar_tensor_tensor(sd[:, j, :], ps_sc[:, sc.slot, :], RDK ** -0.5,
                                                 decay[:, at:at + T], ALU.mult, ALU.mult)\
                            .then_inc(s_sc_free[sc.slot], 1)
                        sc.k += 1
                    elif what == "O":
                        i = arg[0]
                        if i == 0:
                            dve.wait_ge(s_swish, ret.n(1))
                        dve.wait_ge(s_out, START + outs.n(1))
                        dve.tensor_tensor(swish[:, i, :], ps_out[:, outs.slot, 0:RDV], swish[:, i, :],
                                          ALU.mult).then_inc(s_gated, 1)
                        outs.k += 1
                        if i == NT - 1:
                            all_read(dve, s_out_free, outs)
                            inverse(ret_inv, ret_ms, RDV).then_inc(s_rvar, 1)
                            dve.wait_ge(s_rrstd, ret.n(1))
                            for k in range(NT):
                                last = dve.tensor_scalar(swish[:, k, :], swish[:, k, :], ret_rstd[:, k:k + 1],
                                                         None, ALU.mult)
                            last.then_inc(s_rn, 1)
                    elif what == "A":
                        c = arg[0]
                        dve.wait_ge(s_tr, tr.n(1))
                        dve.tensor_copy(ret_t[:, ret_head * 2 + c, :], ps_tr[:, tr.slot, :])\
                            .then_inc(s_tr_free[tr.slot], 1)
                        tr.k += 1
                        if c == 1:
                            ret.k += 1

            def operand_lo(dst, src, hi, scale=None):
                dve.wait_ge(s_hi, t["hi"].n(1))
                if scale is None:
                    ins = dve.tensor_tensor(dst, src, hi.bitcast(F32), ALU.subtract)
                else:
                    ins = dve.scalar_tensor_tensor(dst, src, scale, hi.bitcast(F32), ALU.mult, ALU.subtract)
                t["hi"].k += 1
                return ins

            dve.wait_ge(s_const, 16 * (n_const - 1))
            with rolled(dve, NB, t, PER_BATCH) as b:
                dve.wait_ge(s_ms, b * (2 * NT) + NT)
                inverse(ms_inv, ms, D).then_inc(s_var, 1)
                dve.wait_ge(s_rstd, b * 2 + 1)
                for i in range(NT):
                    dve.tensor_scalar(xt[:, i, :], xt[:, i, :], rstd[:, i:i + 1], None, ALU.mult)\
                        .then_inc(s_xn, 1)
                split_unit(KC * NA)
                tiles = [(i, half) for i in range(NT) for half in range(2)]

                def gained(i, half, which, dst, slot):
                    dve.tensor_tensor(dst, ps_tr[:, slot, :].rearrange("p (c n) -> p c n", c=4),
                                      gain[:, which, 4 * half:4 * half + 4].unsqueeze(2)
                                      .to_broadcast([P, 4, P]), ALU.mult).then_inc(s_tr_free[slot], 1)

                def hidden_operand_lo(i, half):
                    operand_lo(h_lo[:, 4 * half:4 * half + 4, P * i:P * (i + 1)],
                               tmp[t["lo"].k % 2][:, :].rearrange("p (c n) -> p c n", c=4),
                               h_hi[:, 4 * half:4 * half + 4, P * i:P * (i + 1)]).then_inc(s_lo, 1)
                    t["lo"].k += 1

                for n, (i, half) in enumerate(tiles):
                    dve.wait_ge(s_lo, START + t["lo"].n())
                    dve.wait_ge(s_tr, tr.n(1))
                    gained(i, half, 0, tmp[tr.slot][:, :].rearrange("p (c n) -> p c n", c=4), tr.slot)
                    tr.k += 1
                    t["f"].k += 1
                    if n > 0:
                        hidden_operand_lo(*tiles[n - 1])
                hidden_operand_lo(*tiles[-1])

                a, bb = KC * NA, KC * NBC
                run(head_schedule(False, True), "head", (a, a, bb), None, 0)
                run(retention_schedule(), "att", (bb, bb, a), None, 0)
                with rolled(dve, HEADS_LOOP, t, PER_HEAD) as h:
                    run(head_schedule(True, True), "head", (a, a, bb), h, None)
                    run(retention_schedule(), "att", (bb, bb, a), None, h + 1)
                run(head_schedule(True, False), "head", (a,), HP - 1, None)

                all_read(dve, s_out_free, outs)
                all_read(dve, s_tr_free, tr)
                def outputs_lo(chunks):
                    for c in chunks:
                        if c < KC:
                            ins = operand_lo(r_lo[:, c, :], ret_t[:, c, :], r_hi[:, c, :], gain[:, 2, c:c + 1])
                        else:
                            ins = operand_lo(a_lo[:, c - KC, :], att_t[:, c - KC, :], a_hi[:, c - KC, :])
                        ins.then_inc(s_lo, 1)
                        t["lo"].k += 1

                def columns(first, last):
                    for i in range(NT):
                        proj.k += 1
                        if i == 1:
                            split_unit(KC * NC)
                        if first:
                            outputs_lo(range(3 * i, 3 * i + 3))
                    if first:
                        dve.wait_ge(s_gate, b + 1)
                    for u in (2, 3):
                        for i in range(NT):
                            dve.wait_ge(s_proj_free[proj.slot], START + proj.lap - NT + 1)
                            dve.wait_ge(s_proj, START + proj.n(1))
                            g = gate_s[u - 2][:, i, :]
                            dve.tensor_tensor(g, ps_proj[:, proj.slot, 0:NC], g, ALU.mult)\
                                .then_inc(s_proj_free[proj.slot], 1)
                            proj.k += 1
                            if i == 1:
                                split_unit((HP if u == 2 else KC) * NC)
                    if not last:
                        for i in range(NT):
                            proj.k += 1
                            if i == 1:
                                split_unit(KC * NC)

                columns(True, False)
                with rolled(dve, D // NC - 2, t, {"w": 4, "piece": 4, "proj": 16}):
                    columns(False, False)
                columns(False, True)

                for i in range(NT):
                    for half in range(2):
                        dve.wait_ge(s_tr, tr.n(1))
                        blk = (slice(None), slice(4 * half, 4 * half + 4), slice(P * i, P * (i + 1)))
                        operand_lo(h_lo[blk], ps_tr[:, tr.slot, :].rearrange("p (c n) -> p c n", c=4),
                                   h_hi[blk]).then_inc(s_tr_free[tr.slot], 1)
                        tr.k += 1
                for n in range(D // NC):
                    for i in range(NT):
                        if n == 0:
                            dve.wait_ge(s_xr[i], b * 16 + 16)
                        dve.wait_ge(s_proj, START + proj.n(1))
                        dst = xt[:, i, NC * n:NC * (n + 1)]
                        dve.tensor_tensor(dst, ps_proj[:, proj.slot, 0:NC], dst, ALU.add)\
                            .then_inc(s_proj_free[proj.slot], 1)
                        proj.k += 1
                        if i == 1 and n < D // NC - 1:
                            split_unit(KC * NC)

                dve.wait_ge(s_ms, b * (2 * NT) + 2 * NT)
                inverse(ms_inv, ms, D).then_inc(s_var, 1)
                dve.wait_ge(s_rstd, b * 2 + 2)
                for i in range(NT):
                    dve.tensor_scalar(norm2[:, i, :], xt[:, i, :], rstd[:, i:i + 1], None, ALU.mult)\
                        .then_inc(s_n2, 1)
                for i in range(NT):
                    for half in range(2):
                        dve.wait_ge(s_tr, tr.n(1))
                        gained(i, half, 1, norm2_t[:, i % 2, 4 * half:4 * half + 4, :], tr.slot)
                        tr.k += 1
                    dve.wait_ge(s_out, START + outs.n(1))
                    then(dve.reduce_max(soft[:, i:i + 1], ps_out[:, outs.slot, 0:NE], AXX))
                    dve.tensor_scalar(soft[:, i:i + 1], soft[:, i:i + 1], -1.0, None, ALU.mult)\
                        .then_inc(s_shift, 1)
                    dve.wait_ge(s_out_free[outs.slot], START + outs.lap + 1)
                    outs.k += 1
                    then(dve.reciprocal(soft_inv[:, i:i + 1], soft_sum[:, i:i + 1]))
                    dve.tensor_scalar(aff[:, i, :], aff[:, i, :], soft_inv[:, i:i + 1], None, ALU.mult)\
                        .then_inc(s_aff, 1)
                for i in range(NT):
                    dve.wait_ge(s_tr, tr.n(1))
                    dve.tensor_copy(aff_t[:, bass.ds(b * T + i * P, P)], ps_tr[0:NE, tr.slot, 0:P])\
                        .then_inc(s_tr_free[tr.slot], 1)
                    tr.k += 1

            all_read(dve, s_tr_free, tr)
            then(dve.memset(aff_pad[:, :], 0.0))
            dve.tensor_copy(aff_pad[0:NE, :], aff_t[:, 0:T])
            then(dve.tensor_copy(aff_pad[32:32 + NE, :], aff_t[:, T:2 * T]))
            for r in range(CAP // 8):
                eight = slice(8 * r, 8 * r + 8)
                then(dve.max(best[:, eight], aff_pad[:, :]))
                then(dve.max_index(best_at[:, eight], best[:, eight], aff_pad[:, :]))
                then(dve.match_replace(aff_pad[:, :], best[:, eight], aff_pad[:, :], -1.0))
            dve.tensor_copy(best_f[:, :], best_at[:, :]).then_inc(s_best, 1)
            dve.wait_ge(s_store_x, 16 * NB * NT)
            dve.wait_ge(s_tr, tr.n(1))
            dve.tensor_copy(m_gate[0:CAP, :], ps_tr[0:CAP, tr.slot, 0:NE])
            then(dve.tensor_copy(m_gate[CAP:2 * CAP, :], ps_tr[0:CAP, tr.slot, 32:32 + NE]))
            tr.k += 1
            dve.wait_ge(s_tr, tr.n(1))
            dve.tensor_copy(m_index[0:CAP, :], ps_tr[0:CAP, tr.slot, 0:NE])
            dve.tensor_scalar(m_index[CAP:2 * CAP, :], ps_tr[0:CAP, tr.slot, 32:32 + NE], float(T), None,
                              ALU.add).then_inc(s_route, 1)

            mt = {"raw": Tally(RAW_SLOTS), "slot": Tally(SPLIT_SLOTS), "unit": Tally(), "done": Tally(),
                  "tr": Tally(), "step": Tally()}
            raw, slot, unit, done, mtr, step = mt.values()

            def split_units(n=4):
                for _ in range(n):
                    dve.wait_ge(s_mhi, unit.n(1))
                    dve.tensor_tensor(m_lo[slot.slot][:, :, :], m_raw[raw.slot][:, :, :],
                                      m_hi[slot.slot][:, :, :].bitcast(F32), ALU.subtract)\
                        .then_inc(s_mlo, 1)
                    for x in (raw, slot, unit):
                        x.k += 1

            def hidden_step():
                dve.wait_ge(s_used, done.n())
                dve.wait_ge(s_sg, step.n(1))
                dve.wait_ge(s_mtr, mtr.n())
                dve.tensor_tensor(hid[:, :].rearrange("p (a n) -> p a n", a=2), ps_u[:, :, :],
                                  m_swish[:, :].rearrange("p (a n) -> p a n", a=2), ALU.mult)\
                    .then_inc(s_hid, 1)
                step.k += 1

            def part(a, half):
                return a[:, 4 * half:4 * half + 4, :]

            def hidden_lo():
                for half in range(2):
                    dve.wait_ge(s_thi, mtr.n(1))
                    dve.tensor_tensor(part(hid_lo, half), ps_t[:, half, :].rearrange("p (c n) -> p c n", c=4),
                                      part(hid_hi, half).bitcast(F32), ALU.subtract).then_inc(s_tlo, 1)
                    mtr.k += 1

            def tokens_lo():
                for half in range(2):
                    dve.wait_ge(s_mtr, mtr.n(half + 1))
                    dve.tensor_tensor(m_tmp[half][:, :].rearrange("p (c n) -> p c n", c=4),
                                      ps_t[:, half, :].rearrange("p (c n) -> p c n", c=4),
                                      gain[:, 1, 4 * half:4 * half + 4].unsqueeze(2)
                                      .to_broadcast([P, 4, P]), ALU.mult).then_inc(s_mf, 1)
                for half in range(2):
                    dve.wait_ge(s_thi, mtr.n(1))
                    dve.tensor_tensor(part(xs_lo, half), m_tmp[half][:, :].rearrange("p (c n) -> p c n", c=4),
                                      part(xs_hi, half).bitcast(F32), ALU.subtract).then_inc(s_tlo, 1)
                    mtr.k += 1

            def after():
                done.k += 4

            def expert(last):
                after()
                split_units()
                hidden_lo()
                after()
                split_units()
                hidden_step()
                if not last:
                    tokens_lo()
                after()
                split_units(2 if last else 4)
                if not last:
                    after()
                    split_units()
                hidden_lo()
                if last:
                    split_units(2)
                if not last:
                    after()
                    split_units()
                    hidden_step()
                after()
                if not last:
                    split_units()

            for x in (raw, slot, unit):
                x.k += SPLIT_SLOTS
            tokens_lo()
            after()
            split_units()
            after()
            split_units()
            hidden_step()
            per = {"raw": 24, "slot": 24, "unit": 24, "done": 24, "tr": 6, "step": 2}
            with rolled(dve, NE - 1, mt, per):
                expert(False)
            expert(True)

            dve.wait_ge(s_const, 16 * n_const)
            for i in range(0, NB * NT, 2):
                two = slice(i, i + 2)
                dve.wait_ge(s_ysq, i + 2)
                then(dve.tensor_scalar(y_inv[:, two], y_ms[:, two], 1.0 / D, EPS, ALU.mult, ALU.add))
                dve.reciprocal(y_inv[:, two], y_inv[:, two]).then_inc(s_yvar, 1)
                dve.wait_ge(s_yrstd, i // 2 + 1)
                for k in (i, i + 1):
                    dve.scalar_tensor_tensor(y_tile[:, k, :], y_tile[:, k, :], y_ms[:, k:k + 1],
                                             final_gain[:, :], ALU.mult, ALU.mult).then_inc(s_yout, 1)



def rope_tables():
    f = np.float32
    ret_inv = f(1.0) / np.power(f(10000.0), np.linspace(0.0, 1.0, RDK // 2, dtype=f))
    att_inv = np.power(10000.0, -np.arange(0, DH, 2) / DH).astype(f)
    p, r = np.arange(P)[:, None], np.arange(RES)[None, :]
    ret = ((p + P * r).astype(f)[..., None] * ret_inv).astype(np.float64)
    att = ((RES * p + r).astype(f)[..., None] * att_inv).astype(np.float64)
    return [np.stack([np.cos(a), np.sin(a)], axis=2).astype(f) for a in (ret, att)]


def masks():
    q, k = np.arange(P)[:, None, None], np.arange(P)[None, None, :]
    shift = np.arange(-(RES - 1), RES)[None, :, None]
    near = np.abs(RES * (k - q) + shift) <= WIN0
    first = np.where(near, 0.0, MASKED).reshape(P, 7 * P)
    gap = np.arange(P)[None, :] - np.arange(P)[:, None]
    second = np.where(np.concatenate([np.abs(gap) <= WIN0, gap % RES == 0], axis=1), 0.0, MASKED)
    return first.astype(mybir.dt.np(BF16)), second.astype(mybir.dt.np(BF16))


def distances():
    d = np.arange(7 * P)[None, :] - (NT - 1) * P - np.arange(P)[:, None]
    return np.stack([np.maximum(d, 0), np.maximum(-d, 0)], axis=1).astype(np.float16)



def units(w):
    n, rows, cols = w.shape
    return np.ascontiguousarray(w.reshape(n, rows // P, P, cols).transpose(0, 2, 1, 3).reshape(n, P, -1))


def kernel(**inputs):
    import concourse.bacc as bacc
    from concourse.bass_utils import run_bass_kernel_spmd

    a = {k: np.asarray(v) for k, v in inputs.items()}
    w_in = a["w_in"][0]
    rq, rv, aq = RH * RDK, RH * RDV, NG * HG * DH
    cuts = np.cumsum([0, rq, rq, rv, rv, aq, aq, aq])
    q, k, v, g, xq, xk, xv = (w_in[:, cuts[i]:cuts[i + 1]] for i in range(7))
    gates = w_in[:, cuts[7]:]

    def cols(m, at, n):
        return m[:, at:at + n]

    w_a = units(np.stack([u for h in range(RH) for u in (
        np.concatenate([cols(q, RDK * h, RDK), cols(k, RDK * h, RDK)], axis=1),
        cols(v, RDV * h, RDV), cols(g, RDV * h, RDV))]))
    w_b = units(np.stack([np.concatenate([cols(m, 512 * grp + P * h, P) for m in (xq, xk, xv)], axis=1)
                          for h in range(HP) for grp in range(NG)]))
    w_c = units(np.stack([u for n in range(D // NC) for u in (
        cols(gates, NC * n, NC), cols(gates, D + NC * n, NC), cols(a["w_ret_out"][0], NC * n, NC))]))
    w_ca = units(np.stack([cols(a["w_att_out"][0], NC * n, NC) for n in range(D // NC)]))
    w_d = units(np.stack([cols(a["w_out"][0], NC * n, NC) for n in range(D // NC)]))
    router = np.ascontiguousarray(a["w_router"][0].reshape(KC, P, NE).transpose(1, 0, 2))
    gains = np.ascontiguousarray(np.stack([a[n].reshape(KC, P).T for n in ("norm_mix", "norm_ffn", "ret_norm")],
                                          axis=1))
    decays = np.stack([a["ret_log_decay_fwd"][0], a["ret_log_decay_bwd"][0]], axis=1)
    decays = np.ascontiguousarray(np.broadcast_to(decays[None], (P, RH, 2)))
    final = np.ascontiguousarray(np.broadcast_to(a["norm_final"][None, :], (P, D)))
    x = np.concatenate([a["x_prompt"], a["x_sample"]]).reshape(NB, NT, P, D)
    rope_r, rope_a = rope_tables()
    mask0, mask12 = masks()
    ins = {
        "x": x, "w_a": w_a.reshape(RH, 3, P, KC * NA), "w_b": w_b.reshape(HP, NG, P, KC * NBC),
        "w_c": w_c.reshape(D // NC, 3, P, KC * NC), "w_ca": w_ca, "w_d": w_d, "w_router": router,
        "gains": gains, "decays": decays, "norm_final": final, "w_exp_gate": a["w_exp_gate"][0],
        "w_exp_up": a["w_exp_up"][0], "w_exp_down": a["w_exp_down"][0],
        "ident": np.eye(P, dtype=np.float32), "rope_r": rope_r, "rope_a": rope_a, "mask0": mask0,
        "mask12": mask12, "dist": distances(),
    }
    ins = {f"in_{n}": v for n, v in ins.items()}
    nc = bacc.Bacc("TRN2", target_bir_lowering=False, num_devices=1)
    args = [nc.dram_tensor(n, v.shape, mybir.dt.from_np(v.dtype), kind="ExternalInput").ap()
            for n, v in ins.items()]
    normed = nc.dram_tensor("normed", (NB * T, D), F32, kind="Internal").ap()
    y = nc.dram_tensor("y", (NB * T, D), F32, kind="Internal").ap()
    out = nc.dram_tensor("out", (NB, NT, P, D), F32, kind="ExternalOutput").ap()
    hybrid_encoder(nc, *args, normed, y, out)
    r = run_bass_kernel_spmd(nc, [ins], core_ids=[0])
    got = np.asarray(r.results[0]["out"]).reshape(NB, T, D)
    return got[0:1], got[1:2]
```

```python
from contextlib import ExitStack, contextmanager

import numpy as np

import concourse.bass as bass
from concourse import mybir

F32 = mybir.dt.float32
F32R = mybir.dt.float32r
BF16 = mybir.dt.bfloat16
F16 = mybir.dt.float16
U32 = mybir.dt.uint32
ALU = mybir.AluOpType
ACT = mybir.ActivationFunctionType
AXX = mybir.AxisListType.X

P = 128
D = 1024
KC = D // P
T = 512
NB = 2
NT = T // P
RH, RDK, RDV = 4, 128, 256
NG, HG, DH = 3, 8, 64
HP = HG // 2
NE, FH = 16, 2048
CAP = 2 * T // NE
RES = 4
WIN0 = 64
EPS = 1e-6
MASKED = -1.0e30

NA, NBC, NC = 256, 384, 256
UNIT = KC * NBC
HEADS_LOOP = RH - 1

PIECES = ((0, 3), (3, 6), (6, 8))
PER_HEAD = {"w": 6, "piece": 18, "proj": 24, "tr": 34, "sc": 20, "out": 6, "turn": 16, "rope": 16, "ret": 1,
            "score": 8, "step": 8, "link": 11}
PER_COL = {"w": 4, "piece": 4, "proj": 16, "mix": 4}
PER_BATCH = {"w": 44, "piece": 94, "proj": 176, "tr": 162, "sc": 80, "out": 28, "turn": 64, "rope": 64, "ret": 4,
             "score": 32, "step": 32, "mix": 16, "hi": 28, "lo": 12, "link": 51}

MK = 2
MN = 1024
RAW_SLOTS, SPLIT_SLOTS = 8, 4
EARLY_SPLITS = 3
UNITS = NE * 24

START = 1


class Tally:

    def __init__(self, slots=1):
        self.slots, self.items, self.laps, self.k = slots, 0, 0, 0

    def n(self, more=0):
        return self.items + (self.k + more)

    @property
    def slot(self):
        return self.k % self.slots

    @property
    def lap(self):
        return self.laps + self.k // self.slots


@contextmanager
def rolled(eng, count, tallies, per):
    with eng.Fori(0, count) as i:
        kept = {}
        for name, t in tallies.items():
            step = per.get(name, 0)
            assert step % t.slots == 0, name
            kept[name] = (t.items, t.laps, t.k)
            if step:
                t.items = t.items + i * step
                t.laps = t.laps + i * (step // t.slots)
        yield i
        for name, t in tallies.items():
            items, laps, k = kept[name]
            assert t.k - k == per.get(name, 0), (name, t.k - k, per.get(name, 0))
            t.items, t.laps, t.k = items, laps, k + count * per.get(name, 0)


def head_schedule(att, proj):
    tiles = [(u, i) for u in (range(3) if proj else (3,)) for i in range(NT)]
    out, behind = [], []

    def project(n):
        for _ in range(n):
            if tiles:
                u, i = tiles.pop(0)
                out.append(("P", u, i))
                if i < len(PIECES):
                    out.append(("W", i))
                if behind:
                    out.append(behind.pop(0))
                if u == 0:
                    behind.append(("R", 0, i))

    steps = 2 * NT
    for s in range(steps + 1):
        if att and s == 0:
            project(1)
        if att and s < steps:
            out.append(("S", s))
        if proj or s % 3:
            project(1)
        if att and s == NT + 1:
            out.append(("V", 0))
        if att and s > 0:
            out.append(("T", s - 1))
        project(1 if proj and s % 3 == 0 and s > 0 else 0)
    project(12)
    out.extend(behind)
    if att:
        out.append(("V", 1))
    return out


def retention_schedule():
    extra = {1: ("K", 0), 2: ("K", 1), 3: ("K", 2), 4: ("K", 3), 5: ("O", 0), 6: ("O", 1), 7: ("O", 2),
             8: ("O", 3), 10: ("A", 0), 11: ("A", 1)}
    out, behind = [("G",)], []
    for n in range(NG * NT):
        g, i = divmod(n, NT)
        out.append(("P", g, i))
        if i < len(PIECES):
            out.append(("W", i))
        if n in extra:
            out.append(extra[n])
        if behind:
            out.append(behind.pop(0))
        behind.append(("R", g, i))
    out.extend(behind)
    return out


def hybrid_encoder(nc, x, w_a, w_b, w_c, w_ca, w_d, w_router, gain_c, gain_rows, decays, norm_final,
                   w_gate, w_up, w_down, ident_c, rope_r_c, rope_a_c, mask0_c, mask12_c, dist_c,
                   normed, y, out):
    ctx = ExitStack()
    with ctx:
        base = 16512
        cursor = [base]

        def put(name, shape, dt, at=None):
            size = int(np.prod(shape[1:])) * {F32: 4, F32R: 4, U32: 4, BF16: 2, F16: 2}[dt]
            size = -(-size // 32) * 32
            place = cursor[0] if at is None else at
            if at is None:
                cursor[0] += size
            return nc.alloc_sbuf_tensor_at(name, shape, dt, offset=place), place, size

        ident, _, _ = put("ident", [P, P], F32)
        rope_r, _, _ = put("rope_r", [P, NT, 2, RDK // 2], F32)
        rope_a, _, _ = put("rope_a", [P, RES, 2, DH // 2], F32)
        mask0, _, _ = put("mask0", [P, 7 * P], BF16)
        mask12, _, _ = put("mask12", [P, 2 * P], BF16)
        dist, _, _ = put("dist", [P, 2, 7 * P], F16)
        gain, _, _ = put("gain", [P, KC], F32)
        decay_all, _, _ = put("decay_all", [P, RH, 2], F32)
        router, _, _ = put("router", [P, KC, NE], F32)
        small, small_at, _ = put("small", [P, 64], F32)
        aff_t, _, _ = put("aff_t", [NE, NB * T], F32)
        decay_cur = small[:, 0:2]
        ms = small[:, 4:8]
        rstd = small[:, 8:12]
        top = small[:, 12:16]
        psum_row = small[:, 16:18]
        pinv = small[:, 18:20]
        ret_ms = small[:, 20:24]
        ret_rstd = small[:, 24:28]
        soft = small[:, 28:32]
        soft_sum = small[:, 32:36]
        soft_inv = small[:, 36:40]
        shift = small[:, 40:42]
        ms_inv = small[:, 44:48]
        ret_inv = small[:, 48:52]
        y_ms = small[:, 52:60]
        y_inv = small[:, 4:12]

        h_hi, h_at, h_size = put("h_hi", [P, KC, T], F32R)
        h_lo, _, _ = put("h_lo", [P, KC, T], F32R)
        ret_t, ret_at, _ = put("ret_t", [P, KC, T], F32)
        att_t, att_at, _ = put("att_t", [P, HP, T], F32)
        w_at = cursor[0]
        w_raw = [put(f"w_raw{i}", [P, UNIT], F32)[0] for i in range(2)]
        w_hi = [put(f"w_hi{i}", [P, UNIT], F32R)[0] for i in range(2)]
        w_lo = [put(f"w_lo{i}", [P, UNIT], F32R)[0] for i in range(2)]
        xt, _, _ = put("xt", [P, NT, D], F32, at=ret_at)
        merged, _, _ = put("merged", [P, NT, D], F32, at=ret_at)

        area = cursor[0]
        decay, _, _ = put("decay", [P, 7 * P], F32)
        qk_t = [put(f"qk_t{g}", [P, 2, T], F32)[0] for g in range(NG)]
        v_a = [put(f"v_a{g}", [P, RES, P], F32)[0] for g in range(NG)]
        prob = [put(f"prob{i}", [P, 6 * P], F32)[0] for i in range(2)]
        prob_t, _, _ = put("prob_t", [P, RES + 2, T], F32)
        rqk_t, rqk_at, _ = put("rqk_t", [P, 2, T], F32)
        v_r, _, _ = put("v_r", [P, NT, RDV], F32)
        swish, _, _ = put("swish", [P, NT, RDV], F32)
        sd, _, _ = put("sd", [P, NT, T], F32)
        rot1 = [put(f"rot1_{i}", [P, 256], F32)[0] for i in range(2)]
        rot2 = [put(f"rot2_{i}", [P, 256], F32)[0] for i in range(2)]
        assert cursor[0] <= 229344, cursor[0]
        top_end = cursor[0]

        cursor[0] = area
        r_lo, _, _ = put("r_lo", [P, KC, T], F32R)
        a_hi, _, _ = put("a_hi", [P, HP, T], F32R)
        a_lo, _, _ = put("a_lo", [P, HP, T], F32R)
        cursor[0] = rqk_at
        r_hi, _, _ = put("r_hi", [P, KC, T], F32R)
        gate_s = [put(f"gate_s{i}", [P, NT, NC], F32)[0] for i in range(2)]
        assert cursor[0] <= 229344
        cursor[0] = area
        norm2, _, _ = put("norm2", [P, NT, D], F32)
        norm2_t, _, _ = put("norm2_t", [P, 2, KC, P], F32)
        aff, _, _ = put("aff", [P, NT, NE], F32)
        gain_row, _, _ = put("gain_row", [P, D], F32)
        logit_t, _, _ = put("logit_t", [NE, T], F32)
        aff_pad = [put(f"aff_pad{i}", [48, T], F32)[0] for i in range(2)]
        best, _, _ = put("best", [48, CAP], F32)
        best_at, _, _ = put("best_at", [48, CAP], U32)
        best_f, _, _ = put("best_f", [48, CAP], F32)
        assert cursor[0] <= area + 36864

        cursor[0] = w_at
        m_raw = [put(f"m_raw{i}", [P, MK, MN], F32)[0] for i in range(RAW_SLOTS - 1)]
        y_tile, _, _ = put("y_tile", [P, NB * NT, D], F32, at=w_at)
        m_gate, _, _ = put("m_gate", [P, NE], F32)
        m_index, _, _ = put("m_index", [P, NE], U32)
        gate_now, _, _ = put("gate_now", [P, 8], F32)
        index_get, _, _ = put("index_get", [P, 8], U32)
        index_add, _, _ = put("index_add", [P, 8], U32)
        final_gain, _, _ = put("final_gain", [P, D], F32)
        assert cursor[0] <= area
        cursor[0] = h_at
        m_hi = [put(f"m_hi{i}", [P, MK, MN], F32R)[0] for i in range(SPLIT_SLOTS)]
        assert cursor[0] <= ret_at
        cursor[0] = ret_at
        hid_hi, _, _ = put("hid_hi", [P, KC, P], F32R)
        hid_lo, _, _ = put("hid_lo", [P, KC, P], F32R)
        m_raw.append(put(f"m_raw{RAW_SLOTS - 1}", [P, MK, MN], F32)[0])
        assert cursor[0] <= att_at
        cursor[0] = att_at
        m_lo = [put("m_lo0", [P, MK, MN], F32R)[0]]
        assert cursor[0] <= w_at
        cursor[0] = area + 36864
        m_lo += [put(f"m_lo{i}", [P, MK, MN], F32R)[0] for i in range(1, SPLIT_SLOTS)]
        assert cursor[0] <= 229344
        cursor[0] = area
        xs, _, _ = put("xs", [P, D], F32)
        xs_hi, _, _ = put("xs_hi", [P, KC, P], F32R)
        xs_lo, _, _ = put("xs_lo", [P, KC, P], F32R)
        m_swish, _, _ = put("m_swish", [P, MN], F32)
        hid, _, _ = put("hid", [P, MN], F32)
        scaled, _, _ = put("scaled", [P, D], F32)
        assert cursor[0] <= area + 36864

        bank = [ctx.enter_context(nc.psum_tensor(f"bank{i}", [P, 2, 512], F32)) for i in range(4)]
        ps_proj, ps_tr, ps_sc, ps_out = bank
        ps_g, ps_t, ps_u, ps_d = bank

        def sem(name):
            return ctx.enter_context(nc.semaphore(name))

        s_const = sem("consts_loaded")
        s_x = [sem(f"x_loaded{i}") for i in range(NT)]
        s_xr = [sem(f"x_reloaded{i}") for i in range(NT)]
        s_wraw = [sem(f"weights_loaded{i}") for i in range(2)]
        s_whi = sem("weights_hi")
        s_wlo = [sem(f"weights_lo{i}") for i in range(2)]
        s_proj = sem("tile_projected")
        s_proj_free = [sem(f"projection_read{i}") for i in range(2)]
        s_tr = sem("transposed")
        s_tr_free = [sem(f"transposed_read{i}") for i in range(2)]
        s_sc = sem("scores_done")
        s_sc_free = [sem(f"scores_read{i}") for i in range(2)]
        s_out = sem("outputs_done")
        s_out_free = [sem(f"outputs_read{i}") for i in range(2)]
        s_gated = sem("outputs_gated")
        s_link = sem("vector_step_done")
        s_gain = sem("gain_row_loaded")
        s_ms = sem("mean_square_ready")
        s_var = sem("inverse_variance_ready")
        s_rstd = sem("rstd_ready")
        s_xn = sem("tile_normalised")
        s_hi = sem("operand_hi")
        s_lo = sem("operand_lo")
        s_rope_x = sem("rotation_products")
        s_rope = sem("rotated")
        s_dexp = sem("decay_exponents")
        s_decay = sem("decays_ready")
        s_swish = sem("retention_gate_ready")
        s_rvar = sem("retention_inverse_variance")
        s_rrstd = sem("retention_rstd")
        s_rn = sem("retention_normalised")
        s_sm = sem("masked_scores")
        s_exp = sem("probabilities")
        s_prob = sem("probabilities_scaled")
        s_merged = sem("merged")
        s_gate = sem("first_gate_ready")
        s_n2 = sem("router_tile_normalised")
        s_raff = sem("router_exponentials")
        s_aff = sem("affinities")
        s_store_x = sem("mixed_tokens_stored")
        s_store_n = sem("normalised_tokens_stored")
        s_batch_stored = sem("batch_stored")
        s_best = sem("best_tokens")
        s_route = sem("routes_ready")
        s_mraw = [sem(f"expert_weights_loaded{i}") for i in range(RAW_SLOTS)]
        s_mhi = sem("expert_weights_hi")
        s_mlo = sem("expert_weights_lo")
        s_used = sem("expert_weights_used")
        s_mtr = sem("expert_transposed")
        s_thi = sem("expert_operand_hi")
        s_tlo = sem("expert_operand_lo")
        s_sg = sem("expert_swish")
        s_hid = sem("expert_hidden")
        s_gnow = sem("expert_gate_picked")
        s_igot = sem("expert_index_picked")
        s_gather = sem("tokens_gathered")
        s_scaled = sem("expert_output_scaled")
        s_added = sem("expert_output_added")
        s_added_seen = sem("expert_output_add_seen")

        s_y = [sem(f"result_loaded{i}") for i in range(NB * NT)]
        s_ysq = sem("result_mean_square")
        s_yvar = sem("result_inverse_variance")
        s_yrstd = sem("result_rstd")
        s_yout = sem("result_normalised")
        s_stored = [sem(f"result_stored{i}") for i in range(2)]

        s_apart_sp, s_apart_dve, s_apart_pool, s_apart_pe = (
            sem(f"apart_{n}") for n in ("sync", "vector", "gpsimd", "tensor"))

        n_const = 10
        primed = [*s_wlo, s_batch_stored, s_n2, s_proj, *s_tr_free, s_lo, *s_proj_free, s_out,
                  *s_out_free, *s_sc_free, s_sm, s_merged, s_scaled, s_added_seen]

        def apart(eng, spacer):
            eng.sem_inc(spacer, 1)

        def mixer_tallies():
            return {"w": Tally(2), "proj": Tally(2), "tr": Tally(2), "sc": Tally(2), "out": Tally(2),
                    "turn": Tally(2), "rope": Tally(2), "ret": Tally(), "score": Tally(2),
                    "step": Tally(2), "mix": Tally(), "hi": Tally(), "lo": Tally(),
                    "link": Tally(), "piece": Tally()}

        def some(*names):
            return {k: v for k, v in mixer_tallies().items() if k in names}

        def all_read(eng, frees, t):
            eng.wait_ge(frees[0], START + t.lap + t.slot)
            eng.wait_ge(frees[1], START + t.lap)

        def residual_added(eng, proj, i):
            eng.wait_ge(s_proj_free[i % 2], START + proj.lap - 1 + i // 2)

        def thirds(a, groups):
            return a.rearrange("p (g h d) -> p g h d", g=groups, h=2)

        block = ctx.enter_context(nc.Block())

        @block.sync
        def _(sp):
            for dst, src in ((ident[:, :], ident_c), (rope_r[:, :, :, :], rope_r_c),
                             (rope_a[:, :, :, :], rope_a_c), (mask0[:, :], mask0_c),
                             (mask12[:, :], mask12_c), (dist[:, :, :], dist_c), (gain[:, :], gain_c),
                             (decay_all[:, :, :], decays), (router[:, :, :], w_router)):
                sp.dma_start(dst, src).then_inc(s_const, 16)
            t = {"w": Tally(2)}
            w = t["w"]

            def load_unit(src, size):
                sp.wait_ge(s_wlo[w.slot], START + w.lap)
                sp.dma_start(w_raw[w.slot][:, 0:size], src).then_inc(s_wraw[w.slot], 16)
                w.k += 1

            def load_head(h):
                for u in range(3):
                    load_unit(w_a[h, u], KC * NA)
                for u in range(3):
                    load_unit(w_b[h, u], KC * NBC)

            with rolled(sp, NB, t, PER_BATCH) as b:
                sp.wait_ge(s_batch_stored, START + b)
                sp.wait_ge(s_n2, START + b * NT)
                apart(sp, s_apart_sp)
                for i in range(NT):
                    sp.dma_start(xt[:, i, :], x[b, i]).then_inc(s_x[i], 16)
                    if i == 1:
                        sp.dma_start(gain_row[:, :], gain_rows[0]).then_inc(s_gain, 16)
                load_head(0)
                with rolled(sp, HEADS_LOOP, t, {"w": 6}) as h:
                    load_head(h + 1)
                with rolled(sp, D // NC, t, {"w": 4}) as n:
                    for u in range(3):
                        load_unit(w_c[n, u], KC * NC)
                    load_unit(w_ca[n], HP * NC)
                for n in range(D // NC):
                    load_unit(w_d[n], KC * NC)
                    if n == 1:
                        sp.wait_ge(s_tr, b * PER_BATCH["tr"] + 152)
                        apart(sp, s_apart_sp)
                        for i in range(NT):
                            sp.dma_start(xt[:, i, :], x[b, i]).then_inc(s_xr[i], 16)
                        sp.dma_start(gain_row[:, :], gain_rows[1]).then_inc(s_gain, 16)
            sp.wait_ge(s_proj, START + NB * PER_BATCH["proj"])
            sp.dma_start(final_gain[:, :], norm_final).then_inc(s_const, 16)

            mt = {"raw": Tally(RAW_SLOTS), "unit": Tally()}

            def load_expert_unit(src):
                raw, unit = mt["raw"], mt["unit"]
                if unit.k == RAW_SLOTS - 1:
                    sp.wait_ge(s_store_x, 16 * NB * NT)
                    sp.wait_ge(s_n2, START + NB * NT)
                if unit.k >= RAW_SLOTS:
                    sp.wait_ge(s_mlo, unit.n(1 - RAW_SLOTS))
                    apart(sp, s_apart_sp)
                sp.dma_start(m_raw[raw.slot][:, :, :], src.rearrange("(c p) n -> p c n", p=P))\
                    .then_inc(s_mraw[raw.slot], 16)
                raw.k += 1
                unit.k += 1

            def load_in(weights, e, f):
                for j in range(4):
                    load_expert_unit(weights[e, MK * P * j:MK * P * (j + 1), MN * f:MN * (f + 1)])

            def load_down(e, f):
                for j in range(4):
                    row = MN * f + MK * P * j
                    load_expert_unit(w_down[e, row:row + MK * P, :])

            def load_expert(e, last):
                load_in(w_gate, e, 1)
                load_in(w_up, e, 1)
                load_down(e, 0)
                if not last:
                    load_in(w_gate, e + 1, 0)
                    load_in(w_up, e + 1, 0)
                load_down(e, 1)

            load_in(w_gate, 0, 0)
            load_in(w_up, 0, 0)
            with rolled(sp, NE - 1, mt, {"raw": 24, "unit": 24}) as e:
                load_expert(e, False)
            load_expert(NE - 1, True)

            sp.wait_ge(s_added, 16 * NE)
            sp.wait_ge(s_mlo, UNITS)
            for i in range(NB * NT):
                sp.dma_start(y_tile[:, i, :], y[P * i:P * (i + 1), :]).then_inc(s_y[i], 16)
            for i in range(NB * NT):
                sp.wait_ge(s_yout, i + 1)
                sp.dma_start(out[i // NT, i % NT], y_tile[:, i, :]).then_inc(s_stored[i % 2], 16)
            for i in range(2):
                sp.wait_ge(s_stored[i], 16 * NB * NT // 2)

        @block.gpsimd
        def _(pool):
            for each in primed:
                pool.sem_inc(each, START)
            t = some("turn", "mix", "proj", "w", "piece")
            turn, mix, proj, w, piece = t["turn"], t["mix"], t["proj"], t["w"], t["piece"]

            def add_rotation():
                pool.wait_ge(s_rope_x, turn.n(1))
                pool.tensor_tensor(rot1[turn.slot][:, :], rot1[turn.slot][:, :], rot2[turn.slot][:, :],
                                   ALU.add).then_inc(s_rope, 1)
                turn.k += 1

            def split_piece(size, part):
                lo, hi = PIECES[part]
                cols = slice(size // 8 * lo, size // 8 * hi)
                piece.k += 1
                pool.wait_ge(s_whi, piece.n())
                apart(pool, s_apart_pool)
                ins = pool.tensor_tensor(w_lo[w.slot][:, cols], w_raw[w.slot][:, cols],
                                         w_hi[w.slot][:, cols].bitcast(F32), ALU.subtract)
                if hi == 8:
                    ins.then_inc(s_wlo[w.slot], 1)
                    w.k += 1

            def run(schedule, sizes):
                sizes = list(sizes)
                for what, *arg in schedule:
                    if what == "P" and arg[0] == 0:
                        add_rotation()
                    if what == "P":
                        proj.k += 1
                    if what == "W":
                        split_piece(sizes[0], arg[0])
                        if arg[0] == len(PIECES) - 1:
                            sizes.pop(0)

            def head(att):
                run(head_schedule(att, True), (KC * NA, KC * NA, KC * NBC))
                for _ in range(NG * NT):
                    add_rotation()
                proj.k += NG * NT
                w.k += 3
                piece.k += 3 * len(PIECES)

            def batch(b):
                pool.wait_ge(s_whi, b * PER_BATCH["piece"] + 1)
                apart(pool, s_apart_pool)
                pool.tensor_tensor(w_lo[0][:, 0:KC * NA], w_raw[0][:, 0:KC * NA],
                                   w_hi[0][:, 0:KC * NA].bitcast(F32), ALU.subtract).then_inc(s_wlo[0], 1)
                w.k += 1
                piece.k += 1
                head(False)
                with rolled(pool, HEADS_LOOP, t, PER_HEAD):
                    head(True)
                run(head_schedule(True, False), (KC * NA,))
                proj.k -= NT
                w.k += PER_COL["w"] * (D // NC) - 1 + D // NC - 1
                piece.k += PER_COL["piece"] * (D // NC) - 1 + D // NC - 1
                pool.wait_ge(s_lo, START + b * PER_BATCH["lo"] + 12)
                apart(pool, s_apart_pool)
                with rolled(pool, D // NC, t, {"mix": 4, "proj": 16}) as n:
                    proj.k += 3 * NT
                    for i in range(NT):
                        pool.wait_ge(s_proj_free[proj.slot], START + proj.lap + 1)
                        pool.tensor_tensor(merged[:, i, bass.ds(n * NC, NC)], gate_s[0][:, i, :],
                                           gate_s[1][:, i, :], ALU.add).then_inc(s_merged, 1)
                        mix.k += 1
                        proj.k += 1
                proj.k += NT * (D // NC)
                for i in range(NT):
                    residual_added(pool, proj, i)
                    apart(pool, s_apart_pool)
                    pool.dma_start(y[bass.ds(b * T + i * P, P), :], xt[:, i, :]).then_inc(s_store_x, 16)
                for i in range(NT):
                    pool.wait_ge(s_n2, START + b * NT + i + 1)
                    apart(pool, s_apart_pool)
                    pool.dma_start(normed[bass.ds(b * T + i * P, P), :], norm2[:, i, :])\
                        .then_inc(s_store_n, 16)

            with rolled(pool, NB - 1, t, PER_BATCH) as b:
                batch(b)
                pool.wait_ge(s_store_x, b * (16 * NT) + 16 * NT)
                pool.wait_ge(s_store_n, b * (16 * NT) + 16 * NT)
                pool.sem_inc(s_batch_stored, 1)
            batch(NB - 1)

            for i in range(EARLY_SPLITS):
                pool.wait_ge(s_mhi, i + 1)
                pool.tensor_tensor(m_lo[i][:, :, :], m_raw[i][:, :, :], m_hi[i][:, :, :].bitcast(F32),
                                   ALU.subtract).then_inc(s_mlo, 1)

            pool.wait_ge(s_store_x, 16 * NB * NT)
            pool.wait_ge(s_store_n, 16 * NB * NT)
            pool.wait_ge(s_route, 1)

            def gather(e, nth):
                pool.tensor_copy(index_get[:, 0:1], m_index[:, bass.ds(e, 1)]).then_inc(s_igot, 1)
                pool.wait_ge(s_igot, nth)
                apart(pool, s_apart_pool)
                pool.indirect_dma_start(
                    out=xs[:, :], out_offset=None, in_=normed,
                    in_offset=bass.IndirectOffsetOnAxis(ap=index_get[:, 0:1], axis=0)
                ).then_inc(s_gather, 16)

            def add(e, nth):
                pool.tensor_copy(index_add[:, 0:1], m_index[:, bass.ds(e, 1)]).then_inc(s_igot, 1)
                pool.wait_ge(s_igot, nth)
                pool.wait_ge(s_scaled, START + e + 1)
                apart(pool, s_apart_pool)
                pool.indirect_dma_start(
                    out=y, out_offset=bass.IndirectOffsetOnAxis(ap=index_add[:, 0:1], axis=0),
                    in_=scaled[:, :], in_offset=None, compute_op=ALU.add
                ).then_inc(s_added, 16)
                pool.wait_ge(s_added, e * 16 + 16)
                pool.sem_inc(s_added_seen, 1)

            gather(0, 1)
            pool.wait_ge(s_mtr, 2)
            pool.wait_ge(s_gather, 16)
            gather(1, 2)
            with pool.Fori(0, NE - 2) as e:
                pool.wait_ge(s_mtr, e * 6 + 6)
                pool.wait_ge(s_gather, e * 16 + 32)
                gather(e + 2, e * 2 + 3)
                add(e, e * 2 + 4)
            add(NE - 2, 2 * NE - 1)
            add(NE - 1, 2 * NE)

        @block.tensor
        def _(pe):
            t = some("w", "proj", "tr", "sc", "out", "rope", "ret", "step")
            w, proj, tr, sc, outs = t["w"], t["proj"], t["tr"], t["sc"], t["out"]

            def project(cols, chunks, hi, lo, tokens):
                sl = w.slot
                wh = w_hi[sl][:, 0:chunks * cols].rearrange("p (c n) -> p c n", c=chunks)
                wl = w_lo[sl][:, 0:chunks * cols].rearrange("p (c n) -> p c n", c=chunks)
                pe.wait_ge(s_proj_free[proj.slot], START + proj.lap)
                for c in range(chunks):
                    for n, (a, v) in enumerate(((hi, wh), (hi, wl), (lo, wh))):
                        last = pe.matmul(ps_proj[:, proj.slot, 0:cols], a[:, c, tokens], v[:, c, :],
                                         start=c == n == 0, stop=c == chunks - 1 and n == 2)
                last.then_inc(s_proj, 1)
                proj.k += 1

            def unit_ready():
                pe.wait_ge(s_wlo[w.slot], START + w.lap + 1)

            def transposes(ins, rows=P, cols=P):
                pe.wait_ge(s_tr_free[tr.slot], START + tr.lap)
                if rows < P:
                    apart(pe, s_apart_pe)
                for j, a in enumerate(ins):
                    last = pe.transpose(ps_tr[0:cols, tr.slot, rows * j:rows * (j + 1)], a,
                                        ident[0:rows, 0:rows])
                last.then_inc(s_tr, 1)
                tr.k += 1

            def natural(i):
                return slice(i * P, (i + 1) * P)

            def residue(i):
                return slice(i, T, RES)

            def run(schedule, kind):
                rope, step = t["rope"], t["step"]
                earlier = proj.lap + proj.slot, proj.lap
                for what, *arg in schedule:
                    if what == "P":
                        u, i = arg
                        if i == 0:
                            unit_ready()
                        if kind == "head":
                            project(NA, KC, h_hi, h_lo, natural(i))
                        else:
                            project(NBC, KC, h_hi, h_lo, residue(i))
                        if i == NT - 1:
                            w.k += 1
                    elif what == "R":
                        pe.wait_ge(s_rope, rope.n(1))
                        transposes([rot1[rope.slot][:, 0:P], rot1[rope.slot][:, P:2 * P]])
                        rope.k += 1
                    elif what == "S":
                        s = arg[0]
                        a, r = divmod(s, RES)
                        rows = slice(DH * a, DH * (a + 1))
                        if s == 0:
                            all_read(pe, s_tr_free, tr)
                        q = [qk_t[g][rows, 0, natural(r)] for g in range(NG)]
                        pe.wait_ge(s_sc_free[sc.slot], START + sc.lap)
                        pe.matmul(ps_sc[:, sc.slot, :], q[0], qk_t[0][rows, 1, :],
                                  start=True, stop=True).then_inc(s_sc, 1)
                        sc.k += 1
                        pe.wait_ge(s_sc_free[sc.slot], START + sc.lap)
                        for g in (1, 2):
                            last = pe.matmul(ps_sc[:, sc.slot, P * (g - 1):P * g], q[g],
                                             qk_t[g][rows, 1, natural(r)], start=True, stop=True)
                        last.then_inc(s_sc, 1)
                        sc.k += 1
                    elif what == "T":
                        pe.wait_ge(s_prob, step.n(1))
                        p = prob[step.slot]
                        transposes([p[:, natural(j)] for j in range(4)])
                        transposes([p[:, natural(j)] for j in range(4, 6)])
                        step.k += 1
                    elif what == "V":
                        a = arg[0]
                        rows = slice(DH * a, DH * (a + 1))
                        all_read(pe, s_tr_free, tr)
                        if a == 0:
                            pe.wait_ge(s_proj_free[0], START + earlier[0])
                            pe.wait_ge(s_proj_free[1], START + earlier[1])
                        pe.wait_ge(s_out_free[outs.slot], START + outs.lap)
                        for r in range(RES):
                            pe.matmul(ps_out[rows, outs.slot, :], v_a[0][:, r, rows], prob_t[:, r, :],
                                      start=r == 0, stop=False)
                        for g in (1, 2):
                            for r in range(RES):
                                last = pe.matmul(ps_out[rows, outs.slot, natural(r)], v_a[g][:, r, rows],
                                                 prob_t[:, RES + g - 1, natural(r)],
                                                 start=False, stop=g == 2 and r == RES - 1)
                        last.then_inc(s_out, 1)
                        outs.k += 1
                    elif what == "K":
                        j = arg[0]
                        if j == 0:
                            all_read(pe, s_tr_free, tr)
                            pe.wait_ge(s_swish, t["ret"].n(1))
                        pe.wait_ge(s_sc_free[sc.slot], START + sc.lap)
                        pe.matmul(ps_sc[:, sc.slot, :], rqk_t[:, 1, natural(j)], rqk_t[:, 0, :],
                                  start=True, stop=True).then_inc(s_sc, 1)
                        sc.k += 1
                    elif what == "O":
                        i = arg[0]
                        if i == 0:
                            all_read(pe, s_sc_free, sc)
                        pe.wait_ge(s_out_free[outs.slot], START + outs.lap)
                        for j in range(NT):
                            last = pe.matmul(ps_out[:, outs.slot, 0:RDV], sd[:, j, natural(i)], v_r[:, j, :],
                                             start=j == 0, stop=j == NT - 1)
                        last.then_inc(s_out, 1)
                        outs.k += 1
                    elif what == "A":
                        c = arg[0]
                        pe.wait_ge(s_rn, t["ret"].n(1))
                        transposes([swish[:, i, natural(c)] for i in range(NT)])
                        if c == 1:
                            t["ret"].k += 1

            pe.wait_ge(s_const, 16 * (n_const - 1))
            with rolled(pe, NB, t, PER_BATCH) as b:
                for i in range(NT):
                    pe.wait_ge(s_xn, b * NT + i + 1)
                    for half in range(2):
                        transposes([xt[:, i, natural(4 * half + j)] for j in range(4)])
                all_read(pe, s_tr_free, tr)

                run(head_schedule(False, True), "head")
                run(retention_schedule(), "att")
                with rolled(pe, HEADS_LOOP, t, PER_HEAD):
                    run(head_schedule(True, True), "head")
                    run(retention_schedule(), "att")
                run(head_schedule(True, False), "head")

                def columns(last):
                    for u in (1, 2, 3) if last else (1, 2, 3, 0):
                        unit_ready()
                        if u == 2:
                            pe.wait_ge(s_lo, START + b * PER_BATCH["lo"] + 12)
                        for i in range(NT):
                            if u < 3:
                                a, l = ((h_hi, h_lo), (h_hi, h_lo), (r_hi, r_lo))[u]
                                project(NC, KC, a, l, natural(i))
                            else:
                                project(NC, HP, a_hi, a_lo, natural(i))
                        w.k += 1

                with rolled(pe, D // NC - 1, t, PER_COL):
                    columns(False)
                columns(True)

                pe.wait_ge(s_merged, START + b * PER_BATCH["mix"] + 16)
                for i in range(NT):
                    for half in range(2):
                        transposes([merged[:, i, natural(4 * half + j)] for j in range(4)])
                all_read(pe, s_tr_free, tr)
                for n in range(D // NC):
                    unit_ready()
                    for i in range(NT):
                        project(NC, KC, h_hi, h_lo, natural(i))
                    w.k += 1

                def router_transposes(i):
                    pe.wait_ge(s_n2, START + b * NT + i + 1)
                    for half in range(2):
                        transposes([norm2[:, i, natural(4 * half + j)] for j in range(4)])

                def logits(i, ahead):
                    for free in s_tr_free:
                        pe.wait_ge(free, START + tr.lap - ahead)
                    pe.wait_ge(s_out_free[outs.slot], START + outs.lap)
                    for c in range(KC):
                        last = pe.matmul(ps_out[0:NE, outs.slot, 0:P], router[:, c, :], norm2_t[:, i % 2, c, :],
                                         start=c == 0, stop=c == KC - 1)
                    last.then_inc(s_out, 1)
                    outs.k += 1

                router_transposes(0)
                for i in range(1, NT):
                    router_transposes(i)
                    logits(i - 1, 1)
                logits(NT - 1, 0)
                all_read(pe, s_out_free, outs)
                transposes([logit_t[:, natural(i)] for i in range(NT)], rows=NE)
                pe.wait_ge(s_aff, b + 1)
                transposes([aff[:, i, :] for i in range(NT)], cols=NE)

            for n, a in enumerate((best, best_f)):
                pe.wait_ge(s_best, 1)
                pe.wait_ge(s_tr_free[tr.slot], START + tr.lap)
                pe.transpose(ps_tr[0:CAP, tr.slot, 0:48], a[:, :], ident[0:48, 0:48]).then_inc(s_tr, 1)
                tr.k += 1
            pe.wait_ge(s_route, 1)

            mt = {"unit": Tally(), "slot": Tally(SPLIT_SLOTS), "tr": Tally(), "step": Tally(), "op": Tally()}
            unit, slot, mtr, step, op = mt["unit"], mt["slot"], mt["tr"], mt["step"], mt["op"]

            def use(ps, hi, lo, chunk, first, last):
                pe.wait_ge(s_mlo, unit.n(1))
                wh, wl = m_hi[slot.slot], m_lo[slot.slot]
                for k in range(MK):
                    for n, (a, v) in enumerate(((hi, wh), (hi, wl), (lo, wh))):
                        for half in range(2):
                            mm = pe.matmul(ps[:, half, :], a[:, chunk + k, :],
                                           v[:, k, 512 * half:512 * (half + 1)],
                                           start=first and k == n == 0,
                                           stop=last and k == MK - 1 and n == 2)
                mm.then_inc(s_used, 1)
                unit.k += 1
                slot.k += 1

            def gate_cols():
                pe.wait_ge(s_sg, step.n())
                for j in range(4):
                    use(ps_g, xs_hi, xs_lo, MK * j, j == 0, j == 3)

            def up_cols():
                pe.wait_ge(s_hid, step.n())
                for j in range(4):
                    use(ps_u, xs_hi, xs_lo, MK * j, j == 0, j == 3)
                step.k += 1

            def expert_transposes(ins):
                for half in range(2):
                    if mtr.k >= 2:
                        pe.wait_ge(s_tlo, mtr.n(-1))
                    for j in range(4):
                        last = pe.transpose(ps_t[:, half, natural(j)], ins[:, natural(4 * half + j)],
                                            ident[:, :])
                    last.then_inc(s_mtr, 1)
                    mtr.k += 1

            def hidden_transposes(nth):
                pe.wait_ge(s_hid, nth)
                expert_transposes(hid)

            def token_transposes(nth):
                pe.wait_ge(s_gather, nth)
                expert_transposes(xs)

            def operand_ready(later=0):
                pe.wait_ge(s_tlo, mtr.n(-later))

            def down(e, f, later=0):
                operand_ready(later)
                if f == 0:
                    pe.wait_ge(s_scaled, START + e)
                for j in range(4):
                    use(ps_d, hid_hi, hid_lo, MK * j, f == 0 and j == 0, f == 1 and j == 3)

            def expert(e, last):
                gate_cols()
                hidden_transposes(e * 2 + 1)
                up_cols()
                if not last:
                    token_transposes(e * 16 + 32)
                down(e, 0, 0 if last else 2)
                if not last:
                    operand_ready()
                    gate_cols()
                hidden_transposes(e * 2 + 2)
                if not last:
                    up_cols()
                down(e, 1)

            token_transposes(16)
            operand_ready()
            gate_cols()
            up_cols()
            with rolled(pe, NE - 1, mt, {"unit": 24, "slot": 24, "tr": 6, "step": 2}) as e:
                expert(e, False)
            expert(NE - 1, True)

        @block.scalar
        def _(act):
            t = some("w", "proj", "tr", "sc", "out", "turn", "ret", "score", "mix", "hi")
            w, proj, tr, outs = t["w"], t["proj"], t["tr"], t["out"]

            def split_unit(size, part=None):
                lo, hi = (0, 8) if part is None else PIECES[part]
                cols = slice(size // 8 * lo, size // 8 * hi)
                act.wait_ge(s_wraw[w.slot], w.lap * 16 + 16)
                act.wait_ge(s_proj, START + w.items * NT + (NT * (w.k - 1) if w.k >= 2 else 0))
                act.activation(w_hi[w.slot][:, cols], w_raw[w.slot][:, cols], ACT.Copy)\
                    .then_inc(s_whi, 1)
                if hi == 8:
                    w.k += 1

            def operand_hi(dst, src, scale=1.0):
                act.activation(dst, src, ACT.Copy, scale=scale).then_inc(s_hi, 1)
                t["hi"].k += 1

            def run(schedule, kind, sizes, last=False):
                ret, score = t["ret"], t["score"]
                sizes = list(sizes)
                for what, *arg in schedule:
                    if what == "W":
                        split_unit(sizes[0], arg[0])
                        if arg[0] == len(PIECES) - 1:
                            sizes.pop(0)
                    elif what == "P" and arg[0] == 3:
                        i = arg[1]
                        if i == 0:
                            act.wait_ge(s_tr, tr.n())
                        act.wait_ge(s_proj, START + proj.n(1))
                        act.activation(gate_s[0][:, i, :], ps_proj[:, proj.slot, 0:NC], ACT.Copy)\
                            .then_inc(s_proj_free[proj.slot], 1)
                        proj.k += 1
                    elif what == "P" and kind == "head":
                        u, i = arg
                        if u > 0:
                            if (u, i) == (1, 0):
                                act.wait_ge(s_tr, tr.n())
                            act.wait_ge(s_proj, START + proj.n(1))
                            dst = v_r if u == 1 else swish
                            act.activation(dst[:, i, :], ps_proj[:, proj.slot, 0:NA], ACT.Copy)\
                                .then_inc(s_proj_free[proj.slot], 1)
                        else:
                            t["turn"].k += 1
                        proj.k += 1
                    elif what == "P":
                        g, i = arg
                        t["turn"].k += 1
                        if (g, i) == (0, 0):
                            act.wait_ge(s_out, START + outs.n())
                        act.wait_ge(s_rope_x, t["turn"].n())
                        act.activation(v_a[g][:, i, :], ps_proj[:, proj.slot, 2 * P:3 * P], ACT.Copy)\
                            .then_inc(s_proj_free[proj.slot], 1)
                        proj.k += 1
                    elif what == "R":
                        u, i = arg
                        act.wait_ge(s_tr, tr.n(1))
                        dst = rqk_t if kind == "head" else qk_t[u]
                        act.activation(dst[:, :, P * i:P * (i + 1)],
                                       ps_tr[:, tr.slot, 0:2 * P].rearrange("p (a n) -> p a n", a=2),
                                       ACT.Copy).then_inc(s_tr_free[tr.slot], 1)
                        tr.k += 1
                    elif what == "S":
                        i = score.slot
                        act.wait_ge(s_sm, START + score.n(1))
                        act.activation(prob[i][:, :], prob[i][:, :], ACT.Exp, bias=shift[:, i:i + 1],
                                       scale=DH ** -0.5, accum_out=psum_row[:, i:i + 1]).then_inc(s_exp, 1)
                        score.k += 1
                        t["sc"].k += 2
                        if last:
                            if arg[0] == 0:
                                all_read(act, s_tr_free, tr)
                                act.wait_ge(s_tr, tr.n())
                            c = arg[0]
                            operand_hi(r_hi[:, c, :], ret_t[:, c, :], gain[:, c:c + 1])
                    elif what == "T":
                        r = arg[0] % RES
                        if r == 0:
                            act.wait_ge(s_out, START + outs.n())
                        act.wait_ge(s_tr, tr.n(1))
                        act.activation(prob_t[:, 0:RES, P * r:P * (r + 1)],
                                       ps_tr[:, tr.slot, :].rearrange("p (a n) -> p a n", a=RES),
                                       ACT.Copy).then_inc(s_tr_free[tr.slot], 1)
                        tr.k += 2
                    elif what == "V":
                        outs.k += 1
                    elif what == "G":
                        act.wait_ge(s_dexp, ret.n(1))
                        act.activation(decay[:, :], decay[:, :], ACT.Exp).then_inc(s_decay, 1)
                        all_read(act, s_proj_free, proj)
                        act.activation(swish[:, :, :], swish[:, :, :], ACT.Silu).then_inc(s_swish, 1)
                    elif what == "K":
                        t["sc"].k += 1
                    elif what == "O":
                        i = arg[0]
                        act.wait_ge(s_gated, ret.n() * NT + (i + 1))
                        act.activation(ps_out[:, outs.slot, 0:RDV], ps_out[:, outs.slot, 0:RDV], ACT.Square,
                                       accum_out=ret_ms[:, i:i + 1]).then_inc(s_out_free[outs.slot], 1)
                        outs.k += 1
                        if i == NT - 1:
                            act.wait_ge(s_rvar, ret.n(1))
                            act.activation(ret_rstd, ret_inv, ACT.Sqrt).then_inc(s_rrstd, 1)
                    elif what == "A":
                        tr.k += 1
                        if arg[0] == 1:
                            ret.k += 1
                assert not sizes

            act.wait_ge(s_const, 16 * (n_const - 1))
            with rolled(act, NB, t, PER_BATCH) as b:
                act.wait_ge(s_batch_stored, START + b)
                def roots(i, nth):
                    act.wait_ge(s_var, nth)
                    act.activation(rstd[:, i - 1:i + 1], ms_inv[:, i - 1:i + 1], ACT.Sqrt).then_inc(s_rstd, 1)

                for i in range(NT):
                    act.wait_ge(s_x[i], b * 16 + 16)
                    act.activation(norm2[:, i, :], xt[:, i, :], ACT.Square, accum_out=ms[:, i:i + 1])\
                        .then_inc(s_ms, 1)
                    if i % 2 == 1:
                        roots(i, b * 4 + 1 + i // 2)
                split_unit(KC * NA)
                def transposed_hi():
                    for i in range(NT):
                        for half in range(2):
                            act.wait_ge(s_tr, tr.n(1))
                            operand_hi(h_hi[:, 4 * half:4 * half + 4, P * i:P * (i + 1)],
                                       ps_tr[:, tr.slot, :].rearrange("p (c n) -> p c n", c=4))
                            tr.k += 1

                transposed_hi()
                a, bb = KC * NA, KC * NBC
                run(head_schedule(False, True), "head", (a, a, bb))
                run(retention_schedule(), "att", (bb, bb, a))
                with rolled(act, HEADS_LOOP, t, PER_HEAD):
                    run(head_schedule(True, True), "head", (a, a, bb))
                    run(retention_schedule(), "att", (bb, bb, a))
                assert 2 * NT == KC
                run(head_schedule(True, False), "head", (a,), last=True)

                act.wait_ge(s_out, START + outs.n())
                all_read(act, s_out_free, outs)
                all_read(act, s_tr_free, tr)
                all_read(act, s_proj_free, proj)
                act.activation(gate_s[0][:, :, :], gate_s[0][:, :, :], ACT.Sigmoid).then_inc(s_gate, 1)

                for c in range(HP):
                    operand_hi(a_hi[:, c, :], att_t[:, c, :])

                def gate(u, i):
                    act.wait_ge(s_proj, START + proj.n(1))
                    act.activation(gate_s[u][:, i, :], ps_proj[:, proj.slot, 0:NC], ACT.Sigmoid)\
                        .then_inc(s_proj_free[proj.slot], 1)

                def columns(first, last):
                    for i in range(NT):
                        if not first:
                            act.wait_ge(s_merged, START + t["mix"].n(i + 1 - NT))
                        gate(1, i)
                        proj.k += 1
                        if i == 1:
                            split_unit(KC * NC)
                    for u in (2, 3):
                        for i in range(NT):
                            proj.k += 1
                            if i == 3 - u:
                                split_unit((HP if u == 2 else KC) * NC)
                    if not last:
                        for i in range(NT):
                            act.wait_ge(s_merged, START + t["mix"].n(i + 1))
                            gate(0, i)
                            proj.k += 1
                            if i == 1:
                                split_unit(KC * NC)
                    t["mix"].k += NT

                columns(True, False)
                with rolled(act, D // NC - 2, t, PER_COL):
                    columns(False, False)
                columns(False, True)

                transposed_hi()
                for n in range(D // NC):
                    for i in range(NT):
                        proj.k += 1
                        if i == 1 and n < D // NC - 1:
                            split_unit(KC * NC)

                for i in range(NT):
                    residual_added(act, proj, i)
                    act.activation(norm2[:, i, :], xt[:, i, :], ACT.Square, accum_out=ms[:, i:i + 1])\
                        .then_inc(s_ms, 1)
                    if i % 2 == 1:
                        roots(i, b * 4 + 3 + i // 2)
                def logits_read(i):
                    act.wait_ge(s_out, START + outs.n(1))
                    act.activation(logit_t[:, P * i:P * (i + 1)], ps_out[0:NE, outs.slot, 0:P], ACT.Copy)\
                        .then_inc(s_out_free[outs.slot], 1)
                    outs.k += 1

                for i in range(NT):
                    if i >= 2:
                        logits_read(i - 2)
                    act.wait_ge(s_tr, tr.n(1))
                    act.activation(norm2_t[:, i % 2, 0:4, :], ps_tr[:, tr.slot, :].rearrange("p (c n) -> p c n", c=4),
                                   ACT.Copy).then_inc(s_tr_free[tr.slot], 1)
                    tr.k += 2
                logits_read(NT - 2)
                logits_read(NT - 1)
                act.wait_ge(s_tr_free[tr.slot], START + tr.lap + 1)
                act.activation(aff[:, :, :], aff[:, :, :], ACT.Exp).then_inc(s_raff, 1)
                tr.k += 2

            mt = {"raw": Tally(RAW_SLOTS), "slot": Tally(SPLIT_SLOTS), "unit": Tally(), "done": Tally(),
                  "tr": Tally(), "step": Tally()}
            raw, slot, unit, done, mtr, step = mt.values()

            def split_units(n=4):
                for _ in range(n):
                    act.wait_ge(s_mraw[raw.slot], raw.lap * 16 + 16)
                    if unit.k >= SPLIT_SLOTS:
                        act.wait_ge(s_used, unit.n(1 - SPLIT_SLOTS))
                    act.activation(m_hi[slot.slot][:, :, :], m_raw[raw.slot][:, :, :], ACT.Copy)\
                        .then_inc(s_mhi, 1)
                    for x in (raw, slot, unit):
                        x.k += 1

            def swish_step():
                act.wait_ge(s_used, done.n())
                act.wait_ge(s_hid, step.n())
                act.activation(m_swish[:, :], ps_g[:, :, :], ACT.Silu).then_inc(s_sg, 1)
                step.k += 1

            def transposed_hi(operand):
                for half in range(2):
                    act.wait_ge(s_mtr, mtr.n(1))
                    act.activation(operand[:, 4 * half:4 * half + 4, :], ps_t[:, half, :], ACT.Copy)\
                        .then_inc(s_thi, 1)
                    mtr.k += 1

            def after(units=4):
                done.k += units

            def expert(e, last):
                after()
                split_units()
                swish_step()
                transposed_hi(hid_hi)
                after()
                split_units()
                if not last:
                    transposed_hi(xs_hi)
                after()
                split_units(2 if last else 4)
                if not last:
                    after()
                    split_units()
                    swish_step()
                transposed_hi(hid_hi)
                if last:
                    split_units(2)
                if not last:
                    after()
                    split_units()
                after()
                if not last:
                    split_units()
                act.activation(gate_now[:, 0:1], m_gate[:, bass.ds(e, 1)], ACT.Copy).then_inc(s_gnow, 1)
                act.wait_ge(s_gnow, e + 1)
                act.wait_ge(s_used, done.n())
                act.wait_ge(s_added_seen, START + e)
                act.activation(scaled[:, :], ps_d[:, :, :], ACT.Copy, scale=gate_now[:, 0:1])\
                    .then_inc(s_scaled, 1)

            split_units()
            act.wait_ge(s_route, 1)
            transposed_hi(xs_hi)
            after()
            split_units()
            swish_step()
            after()
            split_units()
            per = {"raw": 24, "slot": 24, "unit": 24, "done": 24, "tr": 6, "step": 2}
            with rolled(act, NE - 1, mt, per) as e:
                expert(e, False)
            expert(NE - 1, True)

            for i in range(NB * NT):
                act.wait_ge(s_y[i], 16)
                if i > 0:
                    act.wait_ge(s_ysq, i)
                act.activation(scaled[:, :], y_tile[:, i, :], ACT.Square, accum_out=y_ms[:, i:i + 1])\
                    .then_inc(s_ysq, 1)
                if i % 2 == 1:
                    act.wait_ge(s_yvar, (i + 1) // 2)
                    act.activation(y_ms[:, i - 1:i + 1], y_inv[:, i - 1:i + 1], ACT.Sqrt)\
                        .then_inc(s_yrstd, 1)

        @block.vector
        def _(dve):
            t = some("w", "piece", "proj", "tr", "sc", "out", "turn", "ret", "score", "step", "hi", "lo",
                     "link")
            w, proj, tr, sc, outs, link = t["w"], t["proj"], t["tr"], t["sc"], t["out"], t["link"]

            def then(ins):
                ins.then_inc(s_link, 1)
                link.k += 1
                dve.wait_ge(s_link, link.n())

            def split_unit(size, part=None):
                lo, hi = (0, 8) if part is None else PIECES[part]
                cols = slice(size // 8 * lo, size // 8 * hi)
                dve.wait_ge(s_whi, t["piece"].n(1))
                ins = dve.tensor_tensor(w_lo[w.slot][:, cols], w_raw[w.slot][:, cols],
                                        w_hi[w.slot][:, cols].bitcast(F32), ALU.subtract)
                t["piece"].k += 1
                if hi == 8:
                    ins.then_inc(s_wlo[w.slot], 1)
                    w.k += 1

            def inverse(dst, src, width):
                then(dve.tensor_scalar(dst, src, 1.0 / width, EPS, ALU.mult, ALU.add))
                return dve.reciprocal(dst, dst)

            def rotate(table, i, groups):
                turn, half = t["turn"], 128 // groups
                dve.wait_ge(s_tr, tr.n())
                dve.wait_ge(s_proj, START + proj.n(1))
                q = ps_proj[:, proj.slot, 0:256]
                wide = q.rearrange("p (g d) -> p g d", d=half)
                a = rot1[turn.slot][:, :].rearrange("p (g d) -> p g d", d=half)
                dve.tensor_tensor(a, wide, table[:, i, 0, :].unsqueeze(1).to_broadcast([P, 2 * groups, half]),
                                  ALU.mult)
                x, y2 = thirds(q, groups), thirds(rot2[turn.slot][:, :], groups)
                sin = table[:, i, 1, :].unsqueeze(1).to_broadcast([P, groups, half])
                dve.scalar_tensor_tensor(y2[:, :, 0, :], x[:, :, 1, :], -1.0, sin, ALU.mult, ALU.mult)
                dve.tensor_tensor(y2[:, :, 1, :], x[:, :, 0, :], sin, ALU.mult).then_inc(s_rope_x, 1)
                turn.k += 1

            def scale_step():
                i = t["step"].slot
                dve.wait_ge(s_exp, t["step"].n(1))
                then(dve.reciprocal(pinv[:, i:i + 1], psum_row[:, i:i + 1]))
                dve.tensor_scalar(prob[i][:, :], prob[i][:, :], pinv[:, i:i + 1], None, ALU.mult)\
                    .then_inc(s_prob, 1)
                t["step"].k += 1

            def run(schedule, kind, sizes, att_head, ret_head):
                ret, score = t["ret"], t["score"]
                sizes = list(sizes)
                for what, *arg in schedule:
                    if what == "W" and kind == "head":
                        t["piece"].k += 1
                        if arg[0] == len(PIECES) - 1:
                            w.k += 1
                            sizes.pop(0)
                    elif what == "W":
                        split_unit(sizes[0], arg[0])
                        if arg[0] == len(PIECES) - 1:
                            sizes.pop(0)
                    elif what == "P" and arg[0] == 3:
                        proj.k += 1
                    elif what == "P" and kind == "head":
                        u, i = arg
                        if u == 0:
                            rotate(rope_r, i, 2)
                            dve.wait_ge(s_rope_x, t["turn"].n())
                            dve.sem_inc(s_proj_free[proj.slot], 1)
                        proj.k += 1
                    elif what == "P":
                        rotate(rope_a, arg[1], 4)
                        proj.k += 1
                    elif what == "R":
                        tr.k += 1
                    elif what == "S":
                        i, r = score.slot, arg[0] % RES
                        dve.wait_ge(s_tr, tr.n())
                        dve.wait_ge(s_sm, START + score.n())
                        dve.wait_ge(s_sc, sc.n(1))
                        apart(dve, s_apart_dve)
                        dve.tensor_tensor_reduce(
                            out=prob[i][:, 0:T], in0=ps_sc[:, sc.slot, :],
                            in1=mask0[:, P * (3 - r):P * (3 - r) + T], scale=1.0, scalar=-3.0e38,
                            op0=ALU.add, op1=ALU.max, accum_out=top[:, 0:1]).then_inc(s_sc_free[sc.slot], 1)
                        sc.k += 1
                        dve.wait_ge(s_sc, sc.n(1))
                        apart(dve, s_apart_dve)
                        dve.tensor_tensor_reduce(
                            out=prob[i][:, T:T + 2 * P], in0=ps_sc[:, sc.slot, 0:2 * P],
                            in1=mask12[:, :], scale=1.0, scalar=-3.0e38,
                            op0=ALU.add, op1=ALU.max, accum_out=top[:, 1:2]).then_inc(s_sc_free[sc.slot], 1)
                        sc.k += 1
                        all_read(dve, s_sc_free, sc)
                        dve.tensor_scalar(shift[:, i:i + 1], top[:, 0:1], top[:, 1:2], -DH ** -0.5,
                                          ALU.max, ALU.mult).then_inc(s_sm, 1)
                        score.k += 1
                        if arg[0] > 0:
                            scale_step()
                    elif what == "T":
                        s = arg[0]
                        r = s % RES
                        if s == 2 * NT - 1:
                            scale_step()
                        if r == 0:
                            dve.wait_ge(s_out, START + outs.n())
                        tr.k += 1
                        dve.wait_ge(s_tr, tr.n(1))
                        dve.tensor_copy(prob_t[:, RES:RES + 2, P * r:P * (r + 1)],
                                        ps_tr[:, tr.slot, 0:2 * P].rearrange("p (a n) -> p a n", a=2))\
                            .then_inc(s_tr_free[tr.slot], 1)
                        tr.k += 1
                    elif what == "V":
                        rows = slice(DH * arg[0], DH * (arg[0] + 1))
                        dve.wait_ge(s_out, START + outs.n(1))
                        dve.tensor_copy(att_t[rows, att_head, :].rearrange("p (t r) -> p r t", r=RES),
                                        ps_out[rows, outs.slot, :].rearrange("p (r t) -> p r t", r=RES))\
                            .then_inc(s_out_free[outs.slot], 1)
                        outs.k += 1
                    elif what == "G":
                        all_read(dve, s_sc_free, sc)
                        then(dve.tensor_copy(decay_cur, decay_all[:, ret_head, :]))
                        then(dve.tensor_scalar(decay[:, :], dist[:, 1, :], decay_cur[:, 1:2], None, ALU.mult))
                        dve.scalar_tensor_tensor(decay[:, :], dist[:, 0, :], decay_cur[:, 0:1], decay[:, :],
                                                 ALU.mult, ALU.add).then_inc(s_dexp, 1)
                    elif what == "K":
                        j = arg[0]
                        if j == 0:
                            dve.wait_ge(s_decay, ret.n(1))
                        dve.wait_ge(s_sc, sc.n(1))
                        at = P * (NT - 1 - j)
                        dve.scalar_tensor_tensor(sd[:, j, :], ps_sc[:, sc.slot, :], RDK ** -0.5,
                                                 decay[:, at:at + T], ALU.mult, ALU.mult)\
                            .then_inc(s_sc_free[sc.slot], 1)
                        sc.k += 1
                    elif what == "O":
                        i = arg[0]
                        if i == 0:
                            dve.wait_ge(s_swish, ret.n(1))
                        dve.wait_ge(s_out, START + outs.n(1))
                        dve.tensor_tensor(swish[:, i, :], ps_out[:, outs.slot, 0:RDV], swish[:, i, :],
                                          ALU.mult).then_inc(s_gated, 1)
                        outs.k += 1
                        if i == NT - 1:
                            all_read(dve, s_out_free, outs)
                            inverse(ret_inv, ret_ms, RDV).then_inc(s_rvar, 1)
                            dve.wait_ge(s_rrstd, ret.n(1))
                            for k in range(NT):
                                last = dve.tensor_scalar(swish[:, k, :], swish[:, k, :], ret_rstd[:, k:k + 1],
                                                         None, ALU.mult)
                            last.then_inc(s_rn, 1)
                    elif what == "A":
                        c = arg[0]
                        dve.wait_ge(s_tr, tr.n(1))
                        dve.tensor_copy(ret_t[:, ret_head * 2 + c, :], ps_tr[:, tr.slot, :])\
                            .then_inc(s_tr_free[tr.slot], 1)
                        tr.k += 1
                        if c == 1:
                            ret.k += 1

            def operand_lo(dst, src, hi, scale=None):
                dve.wait_ge(s_hi, t["hi"].n(1))
                if scale is None:
                    ins = dve.tensor_tensor(dst, src, hi.bitcast(F32), ALU.subtract)
                else:
                    ins = dve.scalar_tensor_tensor(dst, src, scale, hi.bitcast(F32), ALU.mult, ALU.subtract)
                t["hi"].k += 1
                return ins

            dve.wait_ge(s_const, 16 * (n_const - 1))
            with rolled(dve, NB, t, PER_BATCH) as b:
                def inverted(i, nth):
                    dve.wait_ge(s_ms, nth)
                    inverse(ms_inv[:, i:i + 2], ms[:, i:i + 2], D).then_inc(s_var, 1)

                for i in range(0, NT, 2):
                    inverted(i, b * (2 * NT) + i + 2)
                    dve.wait_ge(s_rstd, b * 4 + 1 + i // 2)
                    dve.wait_ge(s_gain, b * 32 + 16)
                    for k in (i, i + 1):
                        dve.scalar_tensor_tensor(xt[:, k, :], xt[:, k, :], rstd[:, k:k + 1], gain_row[:, :],
                                                 ALU.mult, ALU.mult).then_inc(s_xn, 1)
                t["piece"].k += 1
                w.k += 1

                def transposed_lo():
                    for i in range(NT):
                        for half in range(2):
                            dve.wait_ge(s_tr, tr.n(1))
                            blk = (slice(None), slice(4 * half, 4 * half + 4), slice(P * i, P * (i + 1)))
                            operand_lo(h_lo[blk], ps_tr[:, tr.slot, :].rearrange("p (c n) -> p c n", c=4),
                                       h_hi[blk]).then_inc(s_tr_free[tr.slot], 1)
                            tr.k += 1

                transposed_lo()
                a, bb = KC * NA, KC * NBC
                run(head_schedule(False, True), "head", (a, a, bb), None, 0)
                run(retention_schedule(), "att", (bb, bb, a), None, 0)
                with rolled(dve, HEADS_LOOP, t, PER_HEAD) as h:
                    run(head_schedule(True, True), "head", (a, a, bb), h, None)
                    run(retention_schedule(), "att", (bb, bb, a), None, h + 1)
                run(head_schedule(True, False), "head", (a,), HP - 1, None)

                all_read(dve, s_out_free, outs)
                all_read(dve, s_tr_free, tr)
                def outputs_lo(chunks):
                    for c in chunks:
                        if c < KC:
                            ins = operand_lo(r_lo[:, c, :], ret_t[:, c, :], r_hi[:, c, :], gain[:, c:c + 1])
                        else:
                            ins = operand_lo(a_lo[:, c - KC, :], att_t[:, c - KC, :], a_hi[:, c - KC, :])
                        ins.then_inc(s_lo, 1)
                        t["lo"].k += 1

                def columns(first, last):
                    if first:
                        outputs_lo(range(KC + HP))
                    for i in range(NT):
                        proj.k += 1
                        if i == 1:
                            split_unit(KC * NC)
                    if first:
                        dve.wait_ge(s_gate, b + 1)
                    for u in (2, 3):
                        for i in range(NT):
                            dve.wait_ge(s_proj_free[proj.slot], START + proj.lap - NT + 1)
                            dve.wait_ge(s_proj, START + proj.n(1))
                            g = gate_s[u - 2][:, i, :]
                            dve.tensor_tensor(g, ps_proj[:, proj.slot, 0:NC], g, ALU.mult)\
                                .then_inc(s_proj_free[proj.slot], 1)
                            proj.k += 1
                            if i == 3 - u:
                                split_unit((HP if u == 2 else KC) * NC)
                    if not last:
                        for i in range(NT):
                            proj.k += 1
                            if i == 1:
                                split_unit(KC * NC)

                columns(True, False)
                with rolled(dve, D // NC - 2, t, {"w": 4, "piece": 4, "proj": 16}):
                    columns(False, False)
                columns(False, True)

                transposed_lo()
                for n in range(D // NC):
                    for i in range(NT):
                        if n == 0:
                            dve.wait_ge(s_xr[i], b * 16 + 16)
                        dve.wait_ge(s_proj, START + proj.n(1))
                        dst = xt[:, i, NC * n:NC * (n + 1)]
                        dve.tensor_tensor(dst, ps_proj[:, proj.slot, 0:NC], dst, ALU.add)\
                            .then_inc(s_proj_free[proj.slot], 1)
                        proj.k += 1
                        if i == 1 and n < D // NC - 1:
                            split_unit(KC * NC)
                        if i == 2 and n == D // NC - 1:
                            inverted(0, b * (2 * NT) + NT + 2)

                def normalised(i):
                    dve.scalar_tensor_tensor(norm2[:, i, :], xt[:, i, :], rstd[:, i:i + 1], gain_row[:, :],
                                             ALU.mult, ALU.mult).then_inc(s_n2, 1)

                def router_operand(i):
                    if i >= 2:
                        dve.wait_ge(s_out, START + outs.n(i - 1))
                    tr.k += 1
                    dve.wait_ge(s_tr, tr.n(1))
                    dve.tensor_copy(norm2_t[:, i % 2, 4:8, :],
                                    ps_tr[:, tr.slot, :].rearrange("p (c n) -> p c n", c=4))\
                        .then_inc(s_tr_free[tr.slot], 1)
                    tr.k += 1

                dve.wait_ge(s_gain, b * 32 + 32)
                dve.wait_ge(s_rstd, b * 4 + 3)
                normalised(0)
                normalised(1)
                inverted(2, b * (2 * NT) + 2 * NT)
                router_operand(0)
                dve.wait_ge(s_rstd, b * 4 + 4)
                normalised(2)
                normalised(3)
                for i in range(1, NT):
                    router_operand(i)
                outs.k += NT
                dve.wait_ge(s_tr, tr.n(1))
                logit = ps_tr[:, tr.slot, 0:NT * NE].rearrange("p (a n) -> p a n", a=NT)
                then(dve.reduce_max(soft, logit, AXX))
                dve.tensor_tensor(aff[:, :, :], logit, soft.unsqueeze(2).to_broadcast([P, NT, NE]),
                                  ALU.subtract).then_inc(s_tr_free[tr.slot], 1)
                tr.k += 1
                dve.wait_ge(s_raff, b + 1)
                then(dve.reduce_sum(soft_sum, aff[:, :, :], AXX))
                then(dve.reciprocal(soft_inv, soft_sum))
                dve.tensor_tensor(aff[:, :, :], aff[:, :, :], soft_inv.unsqueeze(2).to_broadcast([P, NT, NE]),
                                  ALU.mult).then_inc(s_aff, 1)
                dve.wait_ge(s_tr, tr.n(1))
                dve.tensor_copy(aff_t[:, bass.ds(b * T, T)], ps_tr[0:NE, tr.slot, :])\
                    .then_inc(s_tr_free[tr.slot], 1)
                tr.k += 1

            all_read(dve, s_tr_free, tr)
            then(dve.memset(aff_pad[0][:, :], 0.0))
            dve.tensor_copy(aff_pad[0][0:NE, :], aff_t[:, 0:T])
            then(dve.tensor_copy(aff_pad[0][32:32 + NE, :], aff_t[:, T:2 * T]))
            for r in range(CAP // 8):
                eight = slice(8 * r, 8 * r + 8)
                left, rest = aff_pad[r % 2], aff_pad[1 - r % 2]
                then(dve.max(best[:, eight], left[:, :]))
                ins = dve.max_index(best_at[:, eight], best[:, eight], left[:, :])
                if r < CAP // 8 - 1:
                    ins = dve.match_replace(rest[:, :], best[:, eight], left[:, :], -1.0)
                then(ins)
            dve.tensor_copy(best_f[:, :], best_at[:, :]).then_inc(s_best, 1)
            dve.wait_ge(s_store_x, 16 * NB * NT)
            dve.wait_ge(s_tr, tr.n(1))
            dve.tensor_copy(m_gate[0:CAP, :], ps_tr[0:CAP, tr.slot, 0:NE])
            then(dve.tensor_copy(m_gate[CAP:2 * CAP, :], ps_tr[0:CAP, tr.slot, 32:32 + NE]))
            tr.k += 1
            dve.wait_ge(s_tr, tr.n(1))
            dve.tensor_copy(m_index[0:CAP, :], ps_tr[0:CAP, tr.slot, 0:NE])
            dve.tensor_scalar(m_index[CAP:2 * CAP, :], ps_tr[0:CAP, tr.slot, 32:32 + NE], float(T), None,
                              ALU.add).then_inc(s_route, 1)

            mt = {"raw": Tally(RAW_SLOTS), "slot": Tally(SPLIT_SLOTS), "unit": Tally(), "done": Tally(),
                  "tr": Tally(), "step": Tally()}
            raw, slot, unit, done, mtr, step = mt.values()

            def split_units(n=4):
                for _ in range(n):
                    dve.wait_ge(s_mhi, unit.n(1))
                    dve.tensor_tensor(m_lo[slot.slot][:, :, :], m_raw[raw.slot][:, :, :],
                                      m_hi[slot.slot][:, :, :].bitcast(F32), ALU.subtract)\
                        .then_inc(s_mlo, 1)
                    for x in (raw, slot, unit):
                        x.k += 1

            def hidden_step():
                dve.wait_ge(s_used, done.n())
                dve.wait_ge(s_sg, step.n(1))
                dve.wait_ge(s_mtr, mtr.n())
                dve.tensor_tensor(hid[:, :].rearrange("p (a n) -> p a n", a=2), ps_u[:, :, :],
                                  m_swish[:, :].rearrange("p (a n) -> p a n", a=2), ALU.mult)\
                    .then_inc(s_hid, 1)
                step.k += 1

            def part(a, half):
                return a[:, 4 * half:4 * half + 4, :]

            def transposed_lo(hi, lo):
                for half in range(2):
                    dve.wait_ge(s_thi, mtr.n(1))
                    dve.tensor_tensor(part(lo, half), ps_t[:, half, :].rearrange("p (c n) -> p c n", c=4),
                                      part(hi, half).bitcast(F32), ALU.subtract).then_inc(s_tlo, 1)
                    mtr.k += 1

            def after():
                done.k += 4

            def expert(last):
                after()
                split_units()
                transposed_lo(hid_hi, hid_lo)
                after()
                split_units()
                hidden_step()
                if not last:
                    transposed_lo(xs_hi, xs_lo)
                after()
                split_units(2 if last else 4)
                if not last:
                    after()
                    split_units()
                transposed_lo(hid_hi, hid_lo)
                if last:
                    split_units(2)
                if not last:
                    after()
                    split_units()
                    hidden_step()
                after()
                if not last:
                    split_units()

            dve.wait_ge(s_mlo, EARLY_SPLITS)
            for x in (raw, slot, unit):
                x.k += EARLY_SPLITS
            split_units(SPLIT_SLOTS - EARLY_SPLITS)
            transposed_lo(xs_hi, xs_lo)
            after()
            split_units()
            after()
            split_units()
            hidden_step()
            per = {"raw": 24, "slot": 24, "unit": 24, "done": 24, "tr": 6, "step": 2}
            with rolled(dve, NE - 1, mt, per):
                expert(False)
            expert(True)

            dve.wait_ge(s_const, 16 * n_const)
            for i in range(0, NB * NT, 2):
                two = slice(i, i + 2)
                dve.wait_ge(s_ysq, i + 2)
                then(dve.tensor_scalar(y_inv[:, two], y_ms[:, two], 1.0 / D, EPS, ALU.mult, ALU.add))
                dve.reciprocal(y_inv[:, two], y_inv[:, two]).then_inc(s_yvar, 1)
                dve.wait_ge(s_yrstd, i // 2 + 1)
                for k in (i, i + 1):
                    dve.scalar_tensor_tensor(y_tile[:, k, :], y_tile[:, k, :], y_ms[:, k:k + 1],
                                             final_gain[:, :], ALU.mult, ALU.mult).then_inc(s_yout, 1)



def rope_tables():
    f = np.float32
    ret_inv = f(1.0) / np.power(f(10000.0), np.linspace(0.0, 1.0, RDK // 2, dtype=f))
    att_inv = np.power(10000.0, -np.arange(0, DH, 2) / DH).astype(f)
    p, r = np.arange(P)[:, None], np.arange(RES)[None, :]
    ret = ((p + P * r).astype(f)[..., None] * ret_inv).astype(np.float64)
    att = ((RES * p + r).astype(f)[..., None] * att_inv).astype(np.float64)
    return [np.stack([np.cos(a), np.sin(a)], axis=2).astype(f) for a in (ret, att)]


def masks():
    q, k = np.arange(P)[:, None, None], np.arange(P)[None, None, :]
    shift = np.arange(-(RES - 1), RES)[None, :, None]
    near = np.abs(RES * (k - q) + shift) <= WIN0
    first = np.where(near, 0.0, MASKED).reshape(P, 7 * P)
    gap = np.arange(P)[None, :] - np.arange(P)[:, None]
    second = np.where(np.concatenate([np.abs(gap) <= WIN0, gap % RES == 0], axis=1), 0.0, MASKED)
    return first.astype(mybir.dt.np(BF16)), second.astype(mybir.dt.np(BF16))


def distances():
    d = np.arange(7 * P)[None, :] - (NT - 1) * P - np.arange(P)[:, None]
    return np.stack([np.maximum(d, 0), np.maximum(-d, 0)], axis=1).astype(np.float16)



def units(w):
    n, rows, cols = w.shape
    return np.ascontiguousarray(w.reshape(n, rows // P, P, cols).transpose(0, 2, 1, 3).reshape(n, P, -1))


def kernel(**inputs):
    import concourse.bacc as bacc
    from concourse.bass_utils import run_bass_kernel_spmd

    a = {k: np.asarray(v) for k, v in inputs.items()}
    w_in = a["w_in"][0]
    rq, rv, aq = RH * RDK, RH * RDV, NG * HG * DH
    cuts = np.cumsum([0, rq, rq, rv, rv, aq, aq, aq])
    q, k, v, g, xq, xk, xv = (w_in[:, cuts[i]:cuts[i + 1]] for i in range(7))
    gates = w_in[:, cuts[7]:]

    def cols(m, at, n):
        return m[:, at:at + n]

    w_a = units(np.stack([u for h in range(RH) for u in (
        np.concatenate([cols(q, RDK * h, RDK), cols(k, RDK * h, RDK)], axis=1),
        cols(v, RDV * h, RDV), cols(g, RDV * h, RDV))]))
    w_b = units(np.stack([np.concatenate([cols(m, 512 * grp + P * h, P) for m in (xq, xk, xv)], axis=1)
                          for h in range(HP) for grp in range(NG)]))
    w_c = units(np.stack([u for n in range(D // NC) for u in (
        cols(gates, NC * n, NC), cols(gates, D + NC * n, NC), cols(a["w_ret_out"][0], NC * n, NC))]))
    w_ca = units(np.stack([cols(a["w_att_out"][0], NC * n, NC) for n in range(D // NC)]))
    w_d = units(np.stack([cols(a["w_out"][0], NC * n, NC) for n in range(D // NC)]))
    router = np.ascontiguousarray(a["w_router"][0].reshape(KC, P, NE).transpose(1, 0, 2))
    gain_c = np.ascontiguousarray(a["ret_norm"].reshape(KC, P).T)
    gain_rows = np.ascontiguousarray(np.stack([np.broadcast_to(a[n].reshape(1, D), (P, D))
                                               for n in ("norm_mix", "norm_ffn")]))
    decays = np.stack([a["ret_log_decay_fwd"][0], a["ret_log_decay_bwd"][0]], axis=1)
    decays = np.ascontiguousarray(np.broadcast_to(decays[None], (P, RH, 2)))
    final = np.ascontiguousarray(np.broadcast_to(a["norm_final"][None, :], (P, D)))
    x = np.concatenate([a["x_prompt"], a["x_sample"]]).reshape(NB, NT, P, D)
    rope_r, rope_a = rope_tables()
    mask0, mask12 = masks()
    ins = {
        "x": x, "w_a": w_a.reshape(RH, 3, P, KC * NA), "w_b": w_b.reshape(HP, NG, P, KC * NBC),
        "w_c": w_c.reshape(D // NC, 3, P, KC * NC), "w_ca": w_ca, "w_d": w_d, "w_router": router,
        "gain_c": gain_c, "gain_rows": gain_rows, "decays": decays, "norm_final": final, "w_exp_gate": a["w_exp_gate"][0],
        "w_exp_up": a["w_exp_up"][0], "w_exp_down": a["w_exp_down"][0],
        "ident": np.eye(P, dtype=np.float32), "rope_r": rope_r, "rope_a": rope_a, "mask0": mask0,
        "mask12": mask12, "dist": distances(),
    }
    ins = {f"in_{n}": v for n, v in ins.items()}
    nc = bacc.Bacc("TRN2", target_bir_lowering=False, num_devices=1)
    args = [nc.dram_tensor(n, v.shape, mybir.dt.from_np(v.dtype), kind="ExternalInput").ap()
            for n, v in ins.items()]
    normed = nc.dram_tensor("normed", (NB * T, D), F32, kind="Internal").ap()
    y = nc.dram_tensor("y", (NB * T, D), F32, kind="Internal").ap()
    out = nc.dram_tensor("out", (NB, NT, P, D), F32, kind="ExternalOutput").ap()
    hybrid_encoder(nc, *args, normed, y, out)
    r = run_bass_kernel_spmd(nc, [ins], core_ids=[0])
    got = np.asarray(r.results[0]["out"]).reshape(NB, T, D)
    return got[0:1], got[1:2]
```
